# Optimizing a Trainium2 kernel written in Bass

```python
import math
import jax, jax.numpy as jnp
from jax import lax
import numpy as np

D_MODEL = 1024
BATCH = 1
SEQ = 1024
DEPTH = 2

NSA_HEADS = 8
NSA_KV_HEADS = 2
NSA_GROUP = NSA_HEADS // NSA_KV_HEADS
NSA_HEAD_DIM = 64
NSA_BRANCHES = 3
CMP_BLOCK = 32
CMP_STRIDE = 16
CMP_HIDDEN = 128
SEL_BLOCK = 64
SEL_TOPN = 8
WINDOW = 512
NSA_Q_BLOCK = 64
FORCE_BONUS = 1000.0
GLA_HEADS = 4
GLA_DK = 64
GLA_DV = 128
GLA_GATE_RANK = 16
GLA_TAU = 16.0
GLA_CHUNK = 64
MLA_HEADS = 16
MLA_NOPE = 64
MLA_ROPE = 32
MLA_V = 64
MLA_Q_LORA = 384
MLA_KV_LORA = 256
ROPE_THETA = 10000.0
ATTN_Q_BLOCK = 128
NORM_EPS = 1e-5
NEG_INF = -1e30
DEEPNORM_ALPHA = (2 * DEPTH) ** 0.25
DEEPNORM_BETA = (8 * DEPTH) ** -0.25
N_EVEN = (DEPTH + 1) // 2
N_ODD = DEPTH // 2

NSA_Q_W = NSA_HEADS * NSA_HEAD_DIM
NSA_KV_W = NSA_BRANCHES * 2 * NSA_KV_HEADS * NSA_HEAD_DIM
NSA_GATE_W = NSA_BRANCHES * NSA_HEADS
GLA_QK_W = GLA_HEADS * GLA_DK
GLA_V_W = GLA_HEADS * GLA_DV
EVEN_SPLITS = (NSA_Q_W, NSA_KV_W, NSA_GATE_W, NSA_Q_W, GLA_QK_W, GLA_QK_W, GLA_V_W, GLA_GATE_RANK, GLA_V_W)
EVEN_IN_W = 3368
EVEN_OUT_W = NSA_Q_W + GLA_V_W
MLA_Z_W = MLA_HEADS * MLA_V
ODD_SPLITS = (MLA_Q_LORA, MLA_KV_LORA, MLA_ROPE, MLA_Z_W)
ODD_IN_W = 1696

kernel_name = "nsa_gla_mla_deepnorm_hybrid"

def _split(h, sizes):
    out, off = [], 0
    for s in sizes:
        out.append(h[..., off:off + s])
        off += s
    return out

def _layernorm(x, g, b):
    xf = x.astype(jnp.float32)
    mu = jnp.mean(xf, -1, keepdims=True)
    var = jnp.mean(jnp.square(xf - mu), -1, keepdims=True)
    return ((xf - mu) * lax.rsqrt(var + NORM_EPS) * g + b).astype(x.dtype)

def _rmsnorm(x, g):
    xf = x.astype(jnp.float32)
    y = xf * lax.rsqrt(jnp.mean(jnp.square(xf), -1, keepdims=True) + NORM_EPS)
    return (y * g).astype(x.dtype)

def _alibi_slopes(n):
    return jnp.exp2(-(8.0 / n) * jnp.arange(1, n + 1, dtype=jnp.float32))

def _masked_softmax(s, mask):
    p = jax.nn.softmax(jnp.where(mask, s, NEG_INF), axis=-1)
    return p * mask

def _rope(x, pos):
    d = x.shape[-1]
    half = d // 2
    freqs = jnp.exp(-math.log(ROPE_THETA) * jnp.arange(half, dtype=jnp.float32) * 2.0 / d)
    ang = pos[:, None] * freqs[None, :]
    shape = (ang.shape[0],) + (1,) * (x.ndim - 3) + (half,)
    cos = jnp.cos(ang).reshape(shape).astype(x.dtype)
    sin = jnp.sin(ang).reshape(shape).astype(x.dtype)
    x1, x2 = x[..., :half], x[..., half:]
    return jnp.concatenate([x1 * cos - x2 * sin, x2 * cos + x1 * sin], -1)

def nsa_mixer(q, kv, gate_logits, cmp_pe, cmp_w1, cmp_w2):
    in_dtype = q.dtype
    B, S, _ = q.shape
    G, R, dh = NSA_KV_HEADS, NSA_GROUP, NSA_HEAD_DIM
    q = (q * dh ** -0.5).reshape(B, S, G, R, dh).transpose(0, 2, 3, 1, 4)
    kv = kv.reshape(B, S, NSA_BRANCHES, 2, G, dh).transpose(2, 3, 0, 4, 1, 5)
    slopes = _alibi_slopes(NSA_HEADS).reshape(G, R)[:, :, None, None]
    pos = jnp.arange(S)

    n_cmp = (S - CMP_BLOCK) // CMP_STRIDE + 1
    cmp_start = jnp.arange(n_cmp) * CMP_STRIDE
    cmp_idx = cmp_start[:, None] + jnp.arange(CMP_BLOCK)[None, :]

    def compress(t, j):
        blk = t[:, :, cmp_idx] + cmp_pe[j]
        h = jax.nn.silu(blk.reshape(B, G, n_cmp, CMP_BLOCK * dh) @ cmp_w1[j])
        return h @ cmp_w2[j]

    k_cmp = compress(kv[0, 0], 0)
    v_cmp = compress(kv[0, 1], 1)
    cmp_end = cmp_start + CMP_BLOCK - 1
    dist_c = (pos[:, None] - cmp_end[None, :]).astype(jnp.float32)
    s = jnp.einsum('bgrtd,bgnd->bgrtn', q, k_cmp).astype(jnp.float32) - slopes * dist_c
    p_cmp = _masked_softmax(s, dist_c >= 0)
    o_cmp = jnp.einsum('bgrtn,bgnd->bgrtd', p_cmp.astype(v_cmp.dtype), v_cmp)

    n_sel = S // SEL_BLOCK
    n_top = min(SEL_TOPN, n_sel)
    sel_start = jnp.arange(n_sel) * SEL_BLOCK
    overlap = jnp.clip(
        jnp.minimum(cmp_start[:, None] + CMP_BLOCK, sel_start[None, :] + SEL_BLOCK)
        - jnp.maximum(cmp_start[:, None], sel_start[None, :]), 0).astype(jnp.float32) / CMP_BLOCK
    imp = jnp.einsum('bgrtn,nj->bgtj', p_cmp, overlap)
    cur = (pos // SEL_BLOCK)[:, None]
    jj = jnp.arange(n_sel)[None, :]
    forced = (jj == 0) | (jj == cur) | (jj == cur - 1)
    imp = jnp.where(jj > cur, -1.0, imp + jnp.where(forced, FORCE_BONUS, 0.0))
    _, sel_idx = lax.top_k(imp, n_top)

    k_sel = kv[1, 0].reshape(B, G, n_sel, SEL_BLOCK, dh)
    v_sel = kv[1, 1].reshape(B, G, n_sel, SEL_BLOCK, dh)
    pad = ((0, 0), (0, 0), (WINDOW, 0), (0, 0))
    k_win = jnp.pad(kv[2, 0], pad)
    v_win = jnp.pad(kv[2, 1], pad)

    qb_len = NSA_Q_BLOCK
    n_qb = S // qb_len
    q_blocks = q.reshape(B, G, R, n_qb, qb_len, dh).transpose(3, 0, 1, 2, 4, 5)
    idx_blocks = sel_idx.reshape(B, G, n_qb, qb_len, n_top).transpose(2, 0, 1, 3, 4)
    starts = jnp.arange(n_qb) * qb_len
    bi = jnp.arange(B)[:, None, None, None]
    gi = jnp.arange(G)[None, :, None, None]
    n_keys = n_top * SEL_BLOCK

    def block(args):
        qb, ib, start = args
        tq = start + jnp.arange(qb_len)
        ks = k_sel[bi, gi, ib].reshape(B, G, qb_len, n_keys, dh)
        vs = v_sel[bi, gi, ib].reshape(B, G, qb_len, n_keys, dh)
        kpos = (ib[..., None] * SEL_BLOCK + jnp.arange(SEL_BLOCK)).reshape(B, G, qb_len, n_keys)
        d_s = (tq[:, None] - kpos).astype(jnp.float32)[:, :, None]
        s_s = jnp.einsum('bgrqd,bgqkd->bgrqk', qb, ks).astype(jnp.float32) - slopes * d_s
        p_s = _masked_softmax(s_s, d_s >= 0)
        o_s = jnp.einsum('bgrqk,bgqkd->bgrqd', p_s.astype(vs.dtype), vs)
        kw = lax.dynamic_slice_in_dim(k_win, start, qb_len + WINDOW, axis=2)
        vw = lax.dynamic_slice_in_dim(v_win, start, qb_len + WINDOW, axis=2)
        kp = start - WINDOW + jnp.arange(qb_len + WINDOW)
        d_w = tq[:, None] - kp[None, :]
        mask_w = (d_w >= 0) & (d_w < WINDOW) & (kp[None, :] >= 0)
        s_w = jnp.einsum('bgrqd,bgkd->bgrqk', qb, kw).astype(jnp.float32) - slopes * d_w.astype(jnp.float32)
        p_w = _masked_softmax(s_w, mask_w)
        o_w = jnp.einsum('bgrqk,bgkd->bgrqd', p_w.astype(vw.dtype), vw)
        return o_s, o_w

    o_sel, o_win = lax.map(block, (q_blocks, idx_blocks, starts))
    o_sel = o_sel.transpose(1, 2, 3, 0, 4, 5).reshape(B, G, R, S, dh)
    o_win = o_win.transpose(1, 2, 3, 0, 4, 5).reshape(B, G, R, S, dh)

    g = jax.nn.sigmoid(gate_logits.astype(jnp.float32)).reshape(B, S, NSA_BRANCHES, G, R)
    g = g.transpose(2, 0, 3, 4, 1)[..., None]
    o = g[0] * o_cmp + g[1] * o_sel + g[2] * o_win
    return o.transpose(0, 3, 1, 2, 4).reshape(B, S, NSA_Q_W).astype(in_dtype)

def gla_mixer(q, k, v, gate_low, w_gate, b_gate, norm_g):
    in_dtype = q.dtype
    B, S, _ = q.shape
    H, C = GLA_HEADS, GLA_CHUNK
    n = S // C

    def heads(t, d):
        return t.astype(jnp.float32).reshape(B, n, C, H, d).transpose(0, 3, 1, 2, 4)

    q = heads(q, GLA_DK) * GLA_DK ** -0.5
    k = heads(k, GLA_DK)
    v = heads(v, GLA_DV)
    log_a = jax.nn.log_sigmoid((gate_low @ w_gate + b_gate).astype(jnp.float32)) / GLA_TAU
    b = jnp.cumsum(heads(log_a, GLA_DK), axis=3)
    b_last = b[:, :, :, -1:]
    q_d = q * jnp.exp(b)
    k_d = k * jnp.exp(-b)
    causal = jnp.tril(jnp.ones((C, C), dtype=bool))
    a = jnp.where(causal, jnp.einsum('bhncd,bhnsd->bhncs', q_d, k_d), 0.0)
    o_intra = jnp.einsum('bhncs,bhnse->bhnce', a, v)
    upd = jnp.einsum('bhnsd,bhnse->nbhde', k * jnp.exp(b_last - b), v)
    decay = jnp.exp(b_last[:, :, :, 0]).transpose(2, 0, 1, 3)

    def step(state, inp):
        dec, u = inp
        return dec[..., None] * state + u, state

    _, states = lax.scan(step, jnp.zeros((B, H, GLA_DK, GLA_DV), jnp.float32), (decay, upd))
    o_inter = jnp.einsum('bhncd,nbhde->bhnce', q_d, states)
    o = _rmsnorm(o_intra + o_inter, norm_g)
    return o.transpose(0, 2, 3, 1, 4).reshape(B, S, GLA_V_W).astype(in_dtype)

def mla_mixer(c_q, c_kv, k_rope, q_norm, w_uq, kv_norm, w_ukv):
    B, S, _ = c_q.shape
    H = MLA_HEADS
    pos_f = jnp.arange(S, dtype=jnp.float32)
    q = (_rmsnorm(c_q, q_norm) @ w_uq).reshape(B, S, H, MLA_NOPE + MLA_ROPE)
    q_nope = q[..., :MLA_NOPE]
    q_rope = _rope(q[..., MLA_NOPE:], pos_f)
    kv = (_rmsnorm(c_kv, kv_norm) @ w_ukv).reshape(B, S, H, MLA_NOPE + MLA_V)
    k_nope, v = kv[..., :MLA_NOPE], kv[..., MLA_NOPE:]
    k_rope = _rope(k_rope, pos_f)
    scale = (MLA_NOPE + MLA_ROPE) ** -0.5
    n_qb = S // ATTN_Q_BLOCK
    qn_b = (q_nope * scale).reshape(B, n_qb, ATTN_Q_BLOCK, H, MLA_NOPE).transpose(1, 0, 2, 3, 4)
    qr_b = (q_rope * scale).reshape(B, n_qb, ATTN_Q_BLOCK, H, MLA_ROPE).transpose(1, 0, 2, 3, 4)
    starts = jnp.arange(n_qb) * ATTN_Q_BLOCK
    kpos = jnp.arange(S)

    def block(args):
        qn, qr, start = args
        tq = start + jnp.arange(ATTN_Q_BLOCK)
        s = (jnp.einsum('bqhd,bkhd->bhqk', qn, k_nope)
             + jnp.einsum('bqhd,bkd->bhqk', qr, k_rope)).astype(jnp.float32)
        p = _masked_softmax(s, kpos[None, :] <= tq[:, None])
        return jnp.einsum('bhqk,bkhd->bqhd', p.astype(v.dtype), v)

    o = lax.map(block, (qn_b, qr_b, starts))
    return o.transpose(1, 0, 2, 3, 4).reshape(B, S, MLA_Z_W)

def even_layer(x, w_in, cmp_pe, cmp_w1, cmp_w2, gla_w_gate, gla_b_gate, gla_norm, w_out, ln_g, ln_b):
    h = x @ w_in
    nq, nkv, ng, nz, gq, gk, gv, ga, gz = _split(h, EVEN_SPLITS)
    o_nsa = nsa_mixer(nq, nkv, ng, cmp_pe, cmp_w1, cmp_w2) * jax.nn.silu(nz)
    o_gla = gla_mixer(gq, gk, gv, ga, gla_w_gate, gla_b_gate, gla_norm) * jax.nn.silu(gz)
    y = jnp.concatenate([o_nsa, o_gla], axis=-1) @ w_out
    return _layernorm(DEEPNORM_ALPHA * x + y, ln_g, ln_b)

def odd_layer(x, w_in, q_norm, w_uq, kv_norm, w_ukv, w_out, ln_g, ln_b):
    h = x @ w_in
    cq, ckv, kr, z = _split(h, ODD_SPLITS)
    o = mla_mixer(cq, ckv, kr, q_norm, w_uq, kv_norm, w_ukv) * jax.nn.silu(z)
    y = o @ w_out
    return _layernorm(DEEPNORM_ALPHA * x + y, ln_g, ln_b)

def setup_inputs(seed: int = 0) -> dict:
    key = jax.random.key(seed)
    ks = jax.random.split(key, 19)

    def nrm(k, shape, scale):
        return jax.random.normal(k, shape, jnp.float32) * scale

    E, O = N_EVEN, N_ODD
    return {
        "x": nrm(ks[0], (BATCH, SEQ, D_MODEL), 1.0),
        "e_w_in": nrm(ks[1], (E, D_MODEL, EVEN_IN_W), D_MODEL ** -0.5),
        "e_cmp_pe": nrm(ks[2], (E, 2, CMP_BLOCK, NSA_HEAD_DIM), 0.02),
        "e_cmp_w1": nrm(ks[3], (E, 2, CMP_BLOCK * NSA_HEAD_DIM, CMP_HIDDEN), (CMP_BLOCK * NSA_HEAD_DIM) ** -0.5),
        "e_cmp_w2": nrm(ks[4], (E, 2, CMP_HIDDEN, NSA_HEAD_DIM), CMP_HIDDEN ** -0.5),
        "e_gla_w_gate": nrm(ks[5], (E, GLA_GATE_RANK, GLA_QK_W), GLA_GATE_RANK ** -0.5),
        "e_gla_b_gate": nrm(ks[6], (E, GLA_QK_W), 0.1),
        "e_gla_norm": 1.0 + nrm(ks[7], (E, GLA_DV), 0.02),
        "e_w_out": nrm(ks[8], (E, EVEN_OUT_W, D_MODEL), EVEN_OUT_W ** -0.5 * DEEPNORM_BETA),
        "e_ln_g": 1.0 + nrm(ks[9], (E, D_MODEL), 0.02),
        "e_ln_b": nrm(ks[10], (E, D_MODEL), 0.02),
        "o_w_in": nrm(ks[11], (O, D_MODEL, ODD_IN_W), D_MODEL ** -0.5),
        "o_q_norm": 1.0 + nrm(ks[12], (O, MLA_Q_LORA), 0.02),
        "o_w_uq": nrm(ks[13], (O, MLA_Q_LORA, MLA_HEADS * (MLA_NOPE + MLA_ROPE)), MLA_Q_LORA ** -0.5),
        "o_kv_norm": 1.0 + nrm(ks[14], (O, MLA_KV_LORA), 0.02),
        "o_w_ukv": nrm(ks[15], (O, MLA_KV_LORA, MLA_HEADS * (MLA_NOPE + MLA_V)), MLA_KV_LORA ** -0.5),
        "o_w_out": nrm(ks[16], (O, MLA_Z_W, D_MODEL), MLA_Z_W ** -0.5 * DEEPNORM_BETA),
        "o_ln_g": 1.0 + nrm(ks[17], (O, D_MODEL), 0.02),
        "o_ln_b": nrm(ks[18], (O, D_MODEL), 0.02),
    }

def reference(x, e_w_in, e_cmp_pe, e_cmp_w1, e_cmp_w2, e_gla_w_gate, e_gla_b_gate, e_gla_norm,
              e_w_out, e_ln_g, e_ln_b, o_w_in, o_q_norm, o_w_uq, o_kv_norm, o_w_ukv, o_w_out,
              o_ln_g, o_ln_b):
    for layer in range(DEPTH):
        i = layer // 2
        if layer % 2 == 0:
            x = even_layer(x, e_w_in[i], e_cmp_pe[i], e_cmp_w1[i], e_cmp_w2[i], e_gla_w_gate[i],
                           e_gla_b_gate[i], e_gla_norm[i], e_w_out[i], e_ln_g[i], e_ln_b[i])
        else:
            x = odd_layer(x, o_w_in[i], o_q_norm[i], o_w_uq[i], o_kv_norm[i], o_w_ukv[i],
                          o_w_out[i], o_ln_g[i], o_ln_b[i])
    return x


_drawn_inputs = setup_inputs


def setup_inputs(seed=0):
    import zlib

    import numpy as np

    out = dict(_drawn_inputs(seed))
    spreads = {}
    factors = {'e_cmp_pe': 8.0,
     'e_gla_w_gate': 3.61,
     'e_gla_b_gate': 8.0,
     'e_gla_norm': 8.0,
     'e_ln_g': 2.85,
     'e_ln_b': 2.861,
     'o_q_norm': 8.0,
     'o_kv_norm': 8.0,
     'o_ln_g': 2.877,
     'o_ln_b': 2.903}
    for name, (base, spread) in spreads.items():
        noise = np.random.default_rng([zlib.crc32(name.encode()), seed]).standard_normal(out[name].shape)
        drawn = base * np.exp(spread * noise) if base else spread * noise
        out[name] = __import__('jax').numpy.asarray(drawn.astype(out[name].dtype))
    for name, factor in factors.items():
        out[name] = (out[name] * factor).astype(out[name].dtype)
    return out
```

```python
from contextlib import ExitStack

import numpy as np

import concourse.bass as bass
from concourse import mybir

F32 = mybir.dt.float32
F32R = mybir.dt.float32r
BF16 = mybir.dt.bfloat16
ALU = mybir.AluOpType
ACT = mybir.ActivationFunctionType
AX = mybir.AxisListType

P = 128
SEQ = 1024
DM = 1024
TT = SEQ // P
KT = DM // P
CW = 512
NEG = -1e30
EPS = 1e-5
ALPHA = 4 ** 0.25

DH = 64
NCMP = 64
N_CMP = 63
CMP_BLOCK, CMP_STRIDE = 32, 16
NSEL = 16
WIN_TILES = 4
GC = 64
GLA_H = 4

T_Q, T_KC, T_VC, T_KS, T_KW, T_GQ, T_GK = 0, 4, 5, 6, 7, 8, 10
N_CH = 12
C_VS, C_VW, C_GATE, C_GA, W_MIX = 0, 128, 256, 280, 296

MLA_H, NOPE, ROPE, VD = 16, 64, 32, 64
QL, KVL = 384, 256
QT, KVT = QL // P, KVL // P
MLA_SCALE = 96 ** -0.5
W_LAT = QL + KVL + ROPE


def positive_wait(eng, sem, value):
    if isinstance(value, int) and value <= 0:
        return
    eng.wait_ge(sem, value)


def mm3(eng, out, lhs, rhs, start, stop):
    eng.matmul(out, lhs[0], rhs[0], start=start, stop=False)
    eng.matmul(out, lhs[0], rhs[1], start=False, stop=False)
    return eng.matmul(out, lhs[1], rhs[0], start=False, stop=stop)


def flat(ap):
    return ap.rearrange("p a b -> p (a b)")


class Core:

    def __init__(self, nc, dram):
        self.nc, self.d = nc, dram
        self.sems = []

    def sem(self, name):
        self.sems.append(self.nc.alloc_semaphore(name=name))
        return self.sems[-1]

    def retire_semaphores(self):
        self.nc.clear_and_free_semaphores(self.sems)
        self.nc.all_engine_barrier()
        self.sems = []


class Space:

    def __init__(self, nc, tag):
        self.nc, self.tag, self.ctx = nc, tag, ExitStack()

    def sb(self, name, shape, dt=F32):
        return self.ctx.enter_context(self.nc.sbuf_tensor(f"{self.tag}_{name}", shape, dt))

    def ps(self, name, shape, dt=F32):
        return self.ctx.enter_context(self.nc.psum_tensor(f"{self.tag}_ps_{name}", shape, dt))

    def close(self):
        self.ctx.close()


RAW = 4
WR = 4


def project(core, tag, w_dram, runs, xh, xl, x_raw_dram=None):
    nc = core.nc
    sp = Space(nc, tag)
    raw = sp.sb("w_raw", [P, RAW, CW])
    wh = sp.sb("w_hi", [P, WR, CW], F32R)
    wl = sp.sb("w_lo", [P, WR, CW], F32R)
    xraw = sp.sb("x_raw", [P, 2, SEQ]) if x_raw_dram is not None else None
    so = sp.sb("silu_out", [P, 4, CW])
    ps = sp.ps("acc", [P, TT, CW])

    raw_in = [core.sem(f"{tag}_w_raw_in{s}") for s in range(RAW)]
    hi_ready = core.sem(f"{tag}_w_hi_ready")
    lo_ready = core.sem(f"{tag}_w_lo_ready")
    slice_used = core.sem(f"{tag}_slice_used")
    acc_ready = core.sem(f"{tag}_acc_ready")
    bank_free = core.sem(f"{tag}_bank_free")
    x_in = [core.sem(f"{tag}_x_in{s}") for s in range(2)]
    xh_ready = core.sem(f"{tag}_xh_ready")
    xl_ready = core.sem(f"{tag}_xl_ready")
    silu_ready = core.sem(f"{tag}_silu_ready")
    spilled = [core.sem(f"{tag}_spilled{s}") for s in range(4)]
    EARLY = 3
    order = [(r, r["first"] + i, i) for r in runs for i in range(r["count"])]
    silu_at = {c: n for n, c in enumerate(c for r, c, _ in order if "silu" in r)}

    def each_chunk(eng, slices, tail=None):
        before = None
        for r in runs:
            def one(c, i, prev):
                slices(r, c, i, range(0, EARLY))
                if tail is not None and prev is not None and "silu" in prev[0]:
                    tail(*prev)
                slices(r, c, i, range(EARLY, KT))
            one(r["first"], 0, before)
            if r["count"] > 1:
                with eng.Fori(1, r["count"]) as i:
                    one(i + r["first"], i, None)
            before = (r, r["first"] + r["count"] - 1)
        if tail is not None and "silu" in before[0]:
            tail(*before)

    def wait_bank(eng, c, t):
        if isinstance(c, int) and c - 1 in silu_at:
            eng.wait_ge(silu_ready, 8 * silu_at[c - 1] + t + 1)
        else:
            plain = c - sum(1 for n in silu_at if n < c) if isinstance(c, int) else c
            positive_wait(eng, bank_free, 8 * plain + t + 1 - 8)

    def with_x(c):
        return x_raw_dram is not None and isinstance(c, int) and c == 0

    def wait_split_slot(eng, c, k):
        if k >= WR:
            positive_wait(eng, slice_used, 7 * c + k - WR + 1)
        elif k + KT - WR < KT - 1:
            positive_wait(eng, slice_used, 7 * c - 7 + k + KT - WR + 1)
        else:
            positive_wait(eng, acc_ready, 8 * c)

    with nc.Block(f"{tag}_blk") as block:

        @block.sync
        def _(sync):
            if x_raw_dram is not None:
                for k in range(2):
                    sync.dma_start(xraw[:, k, :], x_raw_dram[k * P:(k + 1) * P, :]).then_inc(x_in[k], 16)

            def load(run, c, i, ks):
                w = run["width"]
                for k in ks:
                    positive_wait(sync, lo_ready, 8 * c + k + 1 - RAW)
                    col = run["col"] + i * CW
                    sync.dma_start(raw[:, k % RAW, 0:w],
                                   w_dram[k * P:(k + 1) * P, bass.ds(col, w)]).then_inc(raw_in[k % RAW], 16)
                    if with_x(c) and k + 2 < KT:
                        sync.wait_ge(xl_ready, k + 1)
                        sync.dma_start(xraw[:, k % 2, :],
                                       x_raw_dram[(k + 2) * P:(k + 3) * P, :]).then_inc(x_in[k % 2], 16)

            def spill(run, c):
                for t in range(TT):
                    sync.wait_ge(silu_ready, 8 * silu_at[c] + t + 1)
                    sync.dma_start(run["silu"](t), so[:, t % 4, :]).then_inc(spilled[t % 4], 16)

            each_chunk(sync, load, spill)
            if silu_at:
                for s in range(4):
                    sync.wait_ge(spilled[s], 16 * (TT // 4) * len(silu_at))

        @block.scalar
        def _(act):
            def hi(run, c, i, ks):
                w = run["width"]
                for k in ks:
                    if with_x(c):
                        act.wait_ge(x_in[k % 2], 16 * (k // 2 + 1))
                        nc.scalar.activation(xh[:, k, :], xraw[:, k % 2, :], ACT.Copy).then_inc(xh_ready, 1)
                    act.wait_ge(raw_in[k % RAW], 16 * (c * (KT // RAW) + k // RAW + 1))
                    wait_split_slot(act, c, k)
                    nc.scalar.activation(wh[:, k % WR, 0:w], raw[:, k % RAW, 0:w], ACT.Copy).then_inc(hi_ready, 1)

            def silus(run, c):
                for t in range(TT):
                    act.wait_ge(acc_ready, 8 * c + t + 1)
                    positive_wait(act, spilled[t % 4], 16 * (2 * silu_at[c] + t // 4))
                    nc.scalar.activation(so[:, t % 4, :], ps[:, t, :], ACT.Silu).then_inc(silu_ready, 1)

            each_chunk(act, hi, silus)

        @block.gpsimd
        def _(pool):
            def lo(run, c, i, ks):
                w = run["width"]
                for k in ks:
                    pool.wait_ge(hi_ready, 8 * c + k + 1)
                    nc.gpsimd.tensor_tensor(wl[:, k % WR, 0:w], raw[:, k % RAW, 0:w],
                                            wh[:, k % WR, 0:w].bitcast(F32), ALU.subtract).then_inc(lo_ready, 1)

            each_chunk(pool, lo)

        @block.tensor
        def _(pe):
            def chunk(run, c, i, ks):
                w = run["width"]
                for k in ks:
                    slot = k % WR
                    pe.wait_ge(lo_ready, 8 * c + k + 1)
                    if with_x(c):
                        pe.wait_ge(xl_ready, k + 1)
                    for t in range(TT):
                        if k == 0:
                            wait_bank(pe, c, t)
                        if run["kind"] == "ch":
                            ct, th = t // 2, t % 2
                            ws = (wh[:, slot, ct * P:(ct + 1) * P], wl[:, slot, ct * P:(ct + 1) * P])
                            xs = (xh[:, k, th * CW:(th + 1) * CW], xl[:, k, th * CW:(th + 1) * CW])
                            last = mm3(pe, ps[:, t, :], ws, xs, k == 0, k == KT - 1)
                        else:
                            xs = (xh[:, k, t * P:(t + 1) * P], xl[:, k, t * P:(t + 1) * P])
                            ws = (wh[:, slot, 0:w], wl[:, slot, 0:w])
                            last = mm3(pe, ps[:, t, 0:w], xs, ws, k == 0, k == KT - 1)
                        if k == KT - 1:
                            last.then_inc(acc_ready, 1)
                    if k < KT - 1:
                        last.then_inc(slice_used, 1)

            each_chunk(pe, chunk)

        @block.vector
        def _(dve):
            def x_lo(run, c, i, ks):
                if with_x(c):
                    for k in ks:
                        dve.wait_ge(xh_ready, k + 1)
                        nc.vector.tensor_tensor(xl[:, k, :], xraw[:, k % 2, :], xh[:, k, :].bitcast(F32),
                                                ALU.subtract).then_inc(xl_ready, 1)
                if "silu" not in run and KT - 1 in ks:
                    for t in range(TT):
                        dve.wait_ge(acc_ready, 8 * c + t + 1)
                        dst, src = run["move"](ps, i, t)
                        nc.vector.tensor_copy(dst, src).then_inc(bank_free, 1)

            each_chunk(dve, x_lo)

    sp.close()


def gla(core, ch, mix, gv, og_dram, gate_dram):
    nc, d = core.nc, core.d
    sp = Space(nc, "gla")
    wg = sp.sb("w_gate", [17, 2 * P])
    ident = sp.sb("ident", [P, P])
    trisuf = sp.sb("tri_suffix", [P, 2 * P])
    gn = sp.sb("norm_g", [P, P])
    ga_t = sp.sb("ga_t", [17, SEQ])
    neg_half = sp.sb("neg_half", [P, GLA_H])
    nabs = sp.sb("exp_neg_abs", [P, 2, 2 * P])
    lnv = sp.sb("softplus", [P, 2, 2 * P])
    lg = sp.sb("log_a", [P, 2, 2 * P])
    eb = sp.sb("exp_b", [P, 2, 2, P])
    enb = sp.sb("exp_neg_b", [P, 2, 2, P])
    es = sp.sb("exp_suffix", [P, 2, 2, P])
    qd = sp.sb("q_d", [P, 2, 2, P])
    kd = sp.sb("k_d", [P, 2, GLA_H, P])
    kk = sp.sb("k_k", [P, 2, 2, P])
    kks = sp.sb("k_k_tok", [P, 2, 2 * P])
    cmask = sp.sb("causal", [P, GLA_H, GC], mybir.dt.int32)
    atm = sp.sb("a_t_masked", [P, 2, GLA_H, GC])
    st = sp.sb("state", [P, 3, 2, 2 * P])
    sq = sp.sb("square", [P, P])
    ss = sp.sb("sum_sq", [P, 2, GLA_H])
    var = sp.sb("var", [P, 2, GLA_H])
    rstd = sp.sb("rstd", [P, 2, GLA_H])
    gz = sp.sb("silu_gz", [P, 2, CW])
    on = sp.sb("o_norm", [P, 2, CW])
    og = sp.sb("o_gated", [P, 2, CW])
    p_ga = sp.ps("ga_pre", [P, CW])
    p_b = sp.ps("cums", [P, 2, 2 * P])
    p_kk = sp.ps("kk_tok", [P, CW])
    p_a = sp.ps("a_t", [P, 2 * GLA_H, GC])[:, 0:GLA_H, :]
    p_o = [sp.ps(f"o{i}", [P, GLA_H, P]) for i in range(2)]
    p_u = [sp.ps(f"upd{i}", [P, 2, 2 * P]) for i in range(2)]

    S = lambda n: core.sem(f"gla_{n}")
    consts_in, gz_in = S("consts_in"), [S("gz_in0"), S("gz_in1")]
    ones_ready, half_ready, st_zero = S("ones_ready"), S("half_ready"), S("state_zero")
    ga_tr, ga_ready, pre_ready = S("ga_transposed"), S("ga_ready"), S("pre_ready")
    nabs_ready, e_ready, ln_ready, lg_ready = S("nabs_ready"), S("e_ready"), S("ln_ready"), S("lg_ready")
    b_ready, exps_ready, dec_ready = S("b_ready"), S("exps_ready"), S("decayed_ready")
    kk_tr, kks_ready = S("kk_transposed"), S("kks_ready")
    a_ready, atm_ready = S("a_ready"), S("atm_ready")
    o_ready, upd_ready, state_ready = S("o_ready"), S("upd_ready"), S("state_ready")
    ss_ready, var_ready, rstd_ready = S("ss_ready"), S("var_ready"), S("rstd_ready")
    on_ready, og_ready = S("on_ready"), S("og_ready")
    og_out = [S("og_out0"), S("og_out1")]
    sq_done = S("sq_done")

    with nc.Block("gla_blk") as block:

        @block.sync
        def _(sync):
            sync.dma_start(wg[:, :], d["gla_wg"]).then_inc(consts_in, 16)
            sync.dma_start(ident[:, :], d["ident"]).then_inc(consts_in, 16)
            sync.dma_start(trisuf[:, :], d["tri_suffix"]).then_inc(consts_in, 16)
            sync.dma_start(gn[:, :], d["gla_norm"]).then_inc(consts_in, 16)
            sync.dma_start(cmask[:, :, :], d["gla_causal"]).then_inc(consts_in, 16)
            for i in range(2):
                sync.dma_start(gz[:, i, :], gate_dram[i, :, CW:2 * CW]).then_inc(gz_in[i], 16)
            for i in range(TT):
                sync.wait_ge(og_ready, i + 1)
                sync.dma_start(og_dram[i, :, :], og[:, i % 2, :]).then_inc(og_out[i % 2], 16)
                if i + 2 < TT:
                    sync.dma_start(gz[:, i % 2, :], gate_dram[i + 2, :, CW:2 * CW]).then_inc(gz_in[i % 2], 16)
            for s in range(2):
                sync.wait_ge(og_out[s], 16 * (TT // 2))

        @block.gpsimd
        def _(pool):
            nc.gpsimd.memset(ga_t[:, :], 1.0).then_inc(ones_ready, 1)
            nc.gpsimd.memset(neg_half[:, :], -0.5).then_inc(half_ready, 1)
            nc.gpsimd.memset(st[:, :, :, :], 0.0).then_inc(st_zero, 1)
            nc.gpsimd.memset(kd[:, :, :, :], 0.0).then_inc(st_zero, 1)
            nc.gpsimd.memset(atm[:, :, :, :], 0.0).then_inc(st_zero, 1)

            def power(i):
                if i == 0:
                    pool.wait_ge(half_ready, 1)
                pool.wait_ge(var_ready, i + 1)
                positive_wait(pool, on_ready, 4 * (i - 1))
                nc.gpsimd.tensor_tensor(rstd[:, i % 2, :], var[:, i % 2, :], neg_half[:, :],
                                        ALU.pow).then_inc(rstd_ready, 1)

            for i in range(TT):
                power(i)

        @block.tensor
        def _(pe):
            pe.wait_ge(consts_in, 80)
            for t in range(TT):
                positive_wait(pe, ga_ready, t - 1)
                pe.transpose((p_ga, p_kk)[t % 2][0:16, 0:P], mix[:, t, C_GA:C_GA + 16],
                             ident[:, :]).then_inc(ga_tr, 1)

            def gates(i):
                if i == 0:
                    pe.wait_ge(ga_ready, TT)
                positive_wait(pe, lg_ready, i)
                pe.matmul(p_ga[:, 0:2 * P], ga_t[:, i * P:(i + 1) * P], wg[:, :], start=True, stop=True).then_inc(pre_ready, 1)

            def sums(i):
                pe.wait_ge(lg_ready, i + 1)
                positive_wait(pe, exps_ready, 3 * i)
                for p in range(2):
                    last = pe.matmul(p_b[:, p, :], lg[:, i % 2, p * P:(p + 1) * P], trisuf[:, :], start=True, stop=True)
                last.then_inc(b_ready, 1)

            def turn_kk(i):
                pe.wait_ge(dec_ready, 4 * i + 4)
                positive_wait(pe, kks_ready, i)
                for p in range(2):
                    last = pe.transpose(p_kk[:, p * P:(p + 1) * P], kk[:, i % 2, p, :], ident[:, :])
                last.then_inc(kk_tr, 1)

            def scores(i):
                positive_wait(pe, atm_ready, i)
                for hf in range(2):
                    for h in range(GLA_H):
                        c = slice(GC * hf, GC * hf + GC)
                        last = pe.matmul(p_a[c, h, :], kd[:, i % 2, h, c], qd[:, i % 2, h // 2, c],
                                         start=True, stop=True, skip_group_check=True)
                last.then_inc(a_ready, 1)

            def products(i):
                o = p_o[i % 2]
                pe.wait_ge(kks_ready, i + 1)
                for hf in range(2):
                    n = 2 * i + hf
                    c = slice(GC * hf, GC * hf + GC)
                    positive_wait(pe, state_ready, 4 * (n - 1))
                    for p in range(2):
                        last = pe.matmul(p_u[n % 2][:, p, :], kks[c, i % 2, p * P:(p + 1) * P],
                                         gv[c, i, p * 2 * P:(p + 1) * 2 * P], start=True, stop=True)
                    last.then_inc(upd_ready, 1)
                pe.wait_ge(atm_ready, i + 1)
                positive_wait(pe, on_ready, 4 * (i - 1))
                for hf in range(2):
                    n = 2 * i + hf
                    c = slice(GC * hf, GC * hf + GC)
                    for h in range(GLA_H):
                        pe.matmul(o[c, h, :], atm[c, i % 2, h, :], gv[c, i, h * P:(h + 1) * P],
                                  start=h == 0, stop=False, skip_group_check=True)
                    positive_wait(pe, state_ready, 4 * n)
                    for p in range(2):
                        last = pe.matmul(o[c, 2 * p:2 * p + 2, :], qd[:, i % 2, p, c], st[:, n % 3, p, :],
                                         start=False, stop=p == 1, skip_group_check=True)
                last.then_inc(o_ready, 1)

            gates(0)
            sums(0)
            for i in range(TT):
                if i + 1 < TT:
                    gates(i + 1)
                turn_kk(i)
                scores(i)
                if i + 1 < TT:
                    sums(i + 1)
                products(i)

        @block.scalar
        def _(act):
            def softplus(i):
                act.wait_ge(pre_ready, i + 1)
                nc.scalar.activation(nabs[:, i % 2, :], p_ga[:, 0:2 * P], ACT.Abs).then_inc(nabs_ready, 1)
                act.wait_ge(nabs_ready, i + 1)
                nc.scalar.activation(nabs[:, i % 2, :], nabs[:, i % 2, :], ACT.Exp, scale=-1.0).then_inc(e_ready, 1)
                act.wait_ge(e_ready, i + 1)
                positive_wait(act, lg_ready, i - 1)
                nc.scalar.activation(lnv[:, i % 2, :], nabs[:, i % 2, :], ACT.Ln, bias=1.0).then_inc(ln_ready, 1)

            def decays(i):
                act.wait_ge(b_ready, i + 1)
                positive_wait(act, dec_ready, 4 * (i - 1))
                positive_wait(act, state_ready, 8 * (i - 1))
                b = p_b[:, :, 0:P]
                nc.scalar.activation(eb[:, i % 2], b, ACT.Exp).then_inc(exps_ready, 1)
                nc.scalar.activation(enb[:, i % 2], b, ACT.Exp, scale=-1.0).then_inc(exps_ready, 1)
                nc.scalar.activation(es[:, i % 2], p_b[:, :, P:2 * P], ACT.Exp).then_inc(exps_ready, 1)

            def copies(i):
                act.wait_ge(kk_tr, i + 1)
                positive_wait(act, upd_ready, 2 * (i - 1))
                nc.scalar.activation(kks[:, i % 2, :], p_kk[:, 0:2 * P], ACT.Copy).then_inc(kks_ready, 1)

            def squares(i):
                act.wait_ge(o_ready, i + 1)
                positive_wait(act, var_ready, i - 1)
                for h in range(GLA_H):
                    positive_wait(act, sq_done, GLA_H * i + h)
                    ins = nc.scalar.activation(sq[:, :], p_o[i % 2][:, h, :], ACT.Square,
                                               accum_out=ss[:, i % 2, h:h + 1])
                    ins.then_inc(sq_done, 1)

            softplus(0)
            decays(0)
            for i in range(TT):
                if i + 1 < TT:
                    softplus(i + 1)
                copies(i)
                if i + 1 < TT:
                    decays(i + 1)
                squares(i)

        @block.vector
        def _(dve):
            dve.wait_ge(ones_ready, 1)
            for t in range(TT):
                dve.wait_ge(ga_tr, t + 1)
                nc.vector.tensor_copy(ga_t[0:16, t * P:(t + 1) * P],
                                      (p_ga, p_kk)[t % 2][0:16, 0:P]).then_inc(ga_ready, 1)

            def log_gate(i):
                dve.wait_ge(pre_ready, i + 1)
                dve.wait_ge(ln_ready, i + 1)
                positive_wait(dve, b_ready, i - 1)
                nc.vector.scalar_tensor_tensor(out=lg[:, i % 2, :], in0=p_ga[:, 0:2 * P], scalar=0.0,
                                               in1=lnv[:, i % 2, :], op0=ALU.min, op1=ALU.subtract).then_inc(lg_ready, 1)

            def decayed(i):
                dve.wait_ge(exps_ready, 3 * i + 3)
                positive_wait(dve, o_ready, i - 1)
                positive_wait(dve, kk_tr, i - 1)
                tok = slice(i * P, (i + 1) * P)
                nc.vector.tensor_tensor(kk[:, i % 2], ch[:, T_GK:T_GK + 2, tok], es[:, i % 2],
                                        ALU.mult).then_inc(dec_ready, 1)
                for q in range(2):
                    r = slice(64 * q, 64 * q + 64)
                    nc.vector.tensor_tensor(kd[r, i % 2, q:GLA_H:2, :], ch[r, T_GK:T_GK + 2, tok], enb[r, i % 2],
                                            ALU.mult).then_inc(dec_ready, 1)
                nc.vector.scalar_tensor_tensor(out=qd[:, i % 2], in0=ch[:, T_GQ:T_GQ + 2, tok], scalar=64 ** -0.5,
                                               in1=eb[:, i % 2], op0=ALU.mult, op1=ALU.mult).then_inc(dec_ready, 1)

            def causal(i):
                dve.wait_ge(a_ready, i + 1)
                positive_wait(dve, o_ready, i - 1)
                nc.vector.copy_predicated(atm[:, i % 2], cmask[:, :, :], p_a[:, :, :]).then_inc(atm_ready, 1)

            def state(i):
                for hf in range(2):
                    n = 2 * i + hf
                    dve.wait_ge(upd_ready, n + 1)
                    positive_wait(dve, o_ready, i)
                    positive_wait(dve, state_ready, 4 * n)
                    for p in range(2):
                        for q in range(2):
                            r = slice(64 * q, 64 * q + 64)
                            dec = eb[r, i % 2, p, GC * hf + GC - 1:GC * hf + GC]
                            nc.vector.scalar_tensor_tensor(
                                out=st[r, (n + 1) % 3, p, q * P:(q + 1) * P],
                                in0=st[r, n % 3, p, q * P:(q + 1) * P], scalar=dec,
                                in1=p_u[n % 2][r, p, q * P:(q + 1) * P], op0=ALU.mult, op1=ALU.add).then_inc(state_ready, 1)

            def norm(i):
                dve.wait_ge(sq_done, GLA_H * (i + 1))
                positive_wait(dve, rstd_ready, i - 1)
                nc.vector.tensor_scalar(var[:, i % 2, :], ss[:, i % 2, :], 1.0 / P, EPS, ALU.mult, ALU.add).then_inc(var_ready, 1)
                dve.wait_ge(rstd_ready, i + 1)
                positive_wait(dve, og_ready, i - 1)
                for h in range(GLA_H):
                    nc.vector.scalar_tensor_tensor(out=on[:, i % 2, h * P:(h + 1) * P], in0=p_o[i % 2][:, h, :],
                                                   scalar=rstd[:, i % 2, h:h + 1], in1=gn[:, :],
                                                   op0=ALU.mult, op1=ALU.mult).then_inc(on_ready, 1)
                dve.wait_ge(on_ready, 4 * (i + 1))
                dve.wait_ge(gz_in[i % 2], 16 * (i // 2 + 1))
                positive_wait(dve, og_out[i % 2], 16 * (i // 2))
                nc.vector.tensor_tensor(og[:, i % 2, :], on[:, i % 2, :], gz[:, i % 2, :], ALU.mult).then_inc(og_ready, 1)

            dve.wait_ge(st_zero, 3)
            dve.wait_ge(consts_in, 80)
            log_gate(0)
            decayed(0)
            for i in range(TT):
                if i + 1 < TT:
                    log_gate(i + 1)
                causal(i)
                state(i)
                if i + 1 < TT:
                    decayed(i + 1)
                norm(i)

    sp.close()


def over(ap, n):
    return ap.unsqueeze(2).broadcast_to([ap.shape[0], ap.shape[1], n])


def compressed(core, ch, mix, gates, onsa, seln):
    nc, d = core.nc, core.d
    sp = Space(nc, "cmp")
    ident = sp.sb("ident", [P, P])
    w1 = sp.sb("w1", [P, 2, CMP_BLOCK // 2, P])
    kz = sp.sb("kv_two_tokens", [P, 2, 3, SEQ])
    w2 = sp.sb("w2", [P, 2, DH])
    bias = sp.sb("alibi_window", [P, 8, 120])
    ovl = sp.sb("overlap", [P, 2 * NSEL])
    valid = sp.sb("valid", [P, 4, 2, NSEL])
    force = sp.sb("force", [P, 4, 2, NSEL])
    hin = sp.sb("h_in", [P, 4, NCMP])
    hex_ = sp.sb("h_exp", [P, 4, NCMP])
    hs = sp.sb("h_silu", [P, 4, NCMP])
    kc = sp.sb("k_cmp", [P, P])
    vc = sp.sb("v_cmp", [P, P])
    s = sp.sb("scores", [P, 2, 8, NCMP])
    pr = sp.sb("probs", [P, 2, 8, NCMP])
    prn = sp.sb("probs_n", [P, 2, 8, NCMP])
    mx = sp.sb("row_max", [P, 2, 8])
    mf = sp.sb("row_max_floor", [P, 2, 8])
    sm = sp.sb("row_sum", [P, 2, 8])
    sf = sp.sb("row_sum_floor", [P, 2, 8])
    ri = sp.sb("row_inv", [P, 2, 8])
    pt = sp.sb("probs_t", [P, 2, 4, P])
    imp = sp.sb("importance", [P, 2, NSEL])
    impf = sp.sb("importance_forced", [P, 2, NSEL])
    top = sp.sb("top8", [P, 2, 8])
    rep = sp.sb("replaced", [P, 2, NSEL])
    same = sp.sb("unselected", [P, 2, NSEL])
    uns = sp.sb("unselected_neg", [P, 2, NSEL])
    p_h = [sp.ps(f"h{b}", [P, CW]) for b in range(4)]
    p_x = [sp.ps(f"x{b}", [P, CW]) for b in range(4)]

    S = lambda n: core.sem(f"cmp_{n}")
    consts_in, pe_in = S("consts_in"), S("pe_in")
    w1_in = [S(f"w1_in{j}") for j in range(2)]
    kz_even, kz_odd = S("kv_even_ready"), S("kv_odd_ready")
    zeroed, h_ready, hin_ready, hexp_ready, h_step = S("zeroed"), S("h_ready"), S("hin_ready"), S("hexp_ready"), S("h_step")
    kvp_ready, kc_ready = S("kv_psum_ready"), S("kc_vc_ready")
    gexp_ready, gate_step = S("gate_exp_ready"), S("gate_step")
    s_ready, sb_ready, m_step, sub_ready, p_ready = S("s_ready"), S("biased"), S("max_step"), S("sub_ready"), S("p_ready")
    r_step, pn_ready, t_ready, pt_ready = S("sum_step"), S("pn_ready"), S("t_ready"), S("pt_ready")
    o_ready, o_used, imp_step = S("o_ready"), S("o_used"), S("imp_step")
    rep_ready, same_ready = S("rep_ready"), S("same_ready")
    uns_ready, selt_ready, sel_ready = S("uns_ready"), S("selt_ready"), S("sel_ready")

    with nc.Block("cmp_blk") as block:

        @block.sync
        def _(sync):
            sync.dma_start(kz[:, :, 2, 0:CMP_BLOCK], d["cmp_pe_t"]).then_inc(pe_in, 16)
            for j in range(2):
                sync.dma_start(w1[:, j], d["cmp_w1"][:, j]).then_inc(w1_in[j], 16)
            for dst, name in ((ident, "ident"), (w2, "cmp_w2"), (bias, "cmp_bias"),
                              (ovl, "overlap"), (valid, "valid"), (force, "force")):
                sync.dma_start(dst[:], d[name]).then_inc(consts_in, 16)

        @block.gpsimd
        def _(pool):
            nc.gpsimd.memset(kz[:, :, 2, CMP_BLOCK:SEQ], 0.0).then_inc(zeroed, 1)
            nc.gpsimd.memset(kc[:, :], 0.0).then_inc(zeroed, 1)
            nc.gpsimd.memset(vc[:, :], 0.0).then_inc(zeroed, 1)
            nc.gpsimd.memset(hs[:, :, :], 0.0).then_inc(zeroed, 1)
            nc.gpsimd.memset(seln[:, :, :], 0.0).then_inc(zeroed, 1)

        @block.tensor
        def _(pe):
            pe.wait_ge(pe_in, 16)
            pe.wait_ge(zeroed, 1)
            for j in range(2):
                pe.wait_ge(w1_in[j], 16)
                pe.wait_ge(kz_even, 2 * j + 2)
                pe.wait_ge(kz_odd, 2 * j + 2)
                for o in range(0, CMP_BLOCK, 2):
                    last = pe.matmul(p_h[j][:, 0:3 * N_CMP], w1[:, j, o // 2, :],
                                     kz[:, j, :, o:o + CMP_STRIDE * (N_CMP - 1) + 1:CMP_STRIDE],
                                     start=o == 0, stop=o == CMP_BLOCK - 2)
                last.then_inc(h_ready, 1)
            pe.wait_ge(consts_in, 16 * 6)
            pe.wait_ge(h_step, 3)
            for g in range(2):
                c = slice(64 * g, 64 * g + 64)
                pe.matmul(p_x[0][c, 0:N_CMP], w2[:, 0, :], hs[:, g, 0:N_CMP], start=True, stop=True)
                last = pe.matmul(p_x[1][c, 0:DH], hs[:, 2 + g, :], w2[:, 1, :], start=True, stop=True)
            last.then_inc(kvp_ready, 1)
            pe.wait_ge(kc_ready, 4)

            def scores(i):
                positive_wait(pe, sb_ready, i - 1)
                for j in range(4):
                    last = pe.matmul(p_h[i % 2][:, j * P:(j + 1) * P], ch[:, T_Q + j, i * P:(i + 1) * P], kc[:, :],
                                     start=True, stop=True)
                last.then_inc(s_ready, 1)

            def turn(i):
                pe.wait_ge(pn_ready, i + 1)
                positive_wait(pe, pt_ready, i)
                for j in range(4):
                    last = pe.transpose(p_h[2][:, j * P:(j + 1) * P],
                                        prn[:, i % 2, 2 * j:2 * j + 2, :], ident[:, :])
                last.then_inc(t_ready, 1)

            def values(i):
                pe.wait_ge(pt_ready, i + 1)
                positive_wait(pe, o_used, i)
                for j in range(4):
                    pe.matmul(p_h[3][:, j * P:(j + 1) * P], pt[:, i % 2, j, :], vc[:, :], start=True, stop=True)
                positive_wait(pe, imp_step, 4 * (i - 4))
                for j in range(4):
                    last = pe.matmul(p_x[2][:, 0:2 * NSEL], pt[:, i % 2, j, :], ovl[:, :], start=j == 0, stop=j == 3)
                last.then_inc(o_ready, 1)

            def turn_selection(i):
                pe.wait_ge(uns_ready, i - 3)
                positive_wait(pe, sel_ready, i - 4)
                for g in range(2):
                    last = pe.transpose(p_x[3][0:NSEL, g * P:(g + 1) * P], uns[:, g, :], ident[:, :])
                last.then_inc(selt_ready, 1)

            scores(0)
            for i in range(TT):
                if i + 1 < TT:
                    scores(i + 1)
                turn(i)
                if i > 4:
                    turn_selection(i - 1)
                values(i)
            turn_selection(TT - 1)

        @block.scalar
        def _(act):
            for j in range(2):
                for g in range(2):
                    nc.scalar.activation(kz[0:64, j, g, :], ch[64 * g:64 * g + 64, T_KC + j, :],
                                         ACT.Copy).then_inc(kz_even, 1)
            nc.scalar.activation(gates[:, :, :], mix[:, :, C_GATE:C_GATE + 24], ACT.Exp, scale=-1.0).then_inc(gexp_ready, 1)
            act.wait_ge(hin_ready, 2)
            nc.scalar.activation(hex_[:, :, 0:N_CMP], hin[:, :, 0:N_CMP], ACT.Exp, scale=-1.0).then_inc(hexp_ready, 1)

            def turned(i):
                act.wait_ge(t_ready, i + 1)
                positive_wait(act, o_ready, i - 1)
                nc.scalar.activation(pt[:, i % 2], p_h[2][:, :].rearrange("p (a b) -> p a b", a=4),
                                     ACT.Copy).then_inc(pt_ready, 1)

            for i in range(TT):
                act.wait_ge(sub_ready, i + 1)
                positive_wait(act, pn_ready, i - 1)
                nc.scalar.activation(pr[:, i % 2], s[:, i % 2], ACT.Exp).then_inc(p_ready, 1)
                if i > 0:
                    turned(i - 1)
            turned(TT - 1)

        @block.vector
        def _(dve):
            for j in range(2):
                for g in range(2):
                    nc.vector.tensor_copy(kz[64:P, j, g, 0:SEQ - 1],
                                          ch[64 * g:64 * g + 64, T_KC + j, 1:SEQ]).then_inc(kz_odd, 1)
            dve.wait_ge(gexp_ready, 1)
            nc.vector.tensor_scalar(gates[:, :, :], gates[:, :, :], 1.0, None, ALU.add).then_inc(gate_step, 1)
            dve.wait_ge(gate_step, 1)
            nc.vector.reciprocal(gates[:, :, :], gates[:, :, :]).then_inc(gate_step, 1)
            dve.wait_ge(zeroed, 5)
            for j in range(2):
                dve.wait_ge(h_ready, j + 1)
                nc.vector.tensor_scalar(hin[:, 2 * j:2 * j + 2, 0:N_CMP],
                                        p_h[j][:, 0:2 * N_CMP].rearrange("p (g n) -> p g n", g=2),
                                        p_h[j][:, 2 * N_CMP:2 * N_CMP + 1], None, ALU.add).then_inc(hin_ready, 1)
            dve.wait_ge(hexp_ready, 1)
            hx = hex_[:, :, 0:N_CMP]
            nc.vector.tensor_scalar(hx, hx, 1.0, None, ALU.add).then_inc(h_step, 1)
            dve.wait_ge(h_step, 1)
            nc.vector.reciprocal(hx, hx).then_inc(h_step, 1)
            dve.wait_ge(h_step, 2)
            nc.vector.tensor_tensor(hs[:, :, 0:N_CMP], hin[:, :, 0:N_CMP], hx, ALU.mult).then_inc(h_step, 1)
            dve.wait_ge(kvp_ready, 1)
            dve.wait_ge(consts_in, 16 * 6)
            for g in range(2):
                c = slice(64 * g, 64 * g + 64)
                nc.vector.tensor_scalar(kc[c, 64 * g:64 * g + N_CMP], p_x[0][c, 0:N_CMP], DH ** -0.5, None,
                                        ALU.mult).then_inc(kc_ready, 1)
                nc.vector.tensor_copy(vc[c, c], p_x[1][c, 0:DH]).then_inc(kc_ready, 1)

            def soft(i):
                b = i % 2
                dve.wait_ge(s_ready, i + 1)
                positive_wait(dve, p_ready, i - 1)
                nc.vector.tensor_tensor(s[:, b], p_h[b][:, :].rearrange("p (a b) -> p a b", a=8),
                                        bias[:, :, 56 - 8 * i:56 - 8 * i + NCMP], ALU.add).then_inc(sb_ready, 1)
                dve.wait_ge(sb_ready, i + 1)
                nc.vector.tensor_reduce(mx[:, b], s[:, b], AX.X, ALU.max).then_inc(m_step, 1)
                dve.wait_ge(m_step, 2 * i + 1)
                nc.vector.tensor_scalar(mf[:, b], mx[:, b], -1e29, None, ALU.max).then_inc(m_step, 1)
                dve.wait_ge(m_step, 2 * i + 2)
                nc.vector.tensor_tensor(s[:, b], s[:, b], over(mf[:, b], NCMP), ALU.subtract).then_inc(sub_ready, 1)

            def normal(i):
                b = i % 2
                dve.wait_ge(p_ready, i + 1)
                nc.vector.tensor_reduce(sm[:, b], pr[:, b], AX.X, ALU.add).then_inc(r_step, 1)
                dve.wait_ge(r_step, 3 * i + 1)
                nc.vector.tensor_scalar(sf[:, b], sm[:, b], 0.5, None, ALU.max).then_inc(r_step, 1)
                dve.wait_ge(r_step, 3 * i + 2)
                nc.vector.reciprocal(ri[:, b], sf[:, b]).then_inc(r_step, 1)
                dve.wait_ge(r_step, 3 * i + 3)
                positive_wait(dve, t_ready, i - 1)
                nc.vector.tensor_tensor(prn[:, b], pr[:, b], over(ri[:, b], NCMP), ALU.mult).then_inc(pn_ready, 1)

            def result(i):
                dve.wait_ge(o_ready, i + 1)
                if i == 0:
                    dve.wait_ge(gate_step, 2)
                nc.vector.tensor_tensor(onsa[:, i, :].rearrange("p (a b) -> p a b", a=8),
                                        p_h[3][:, :].rearrange("p (a b) -> p a b", a=8),
                                        over(gates[:, i, 0:8], DH), ALU.mult).then_inc(o_used, 1)
                if i >= 4:
                    n = 4 * (i - 4)
                    iv = p_x[2][:, 0:2 * NSEL].rearrange("p (a b) -> p a b", a=2)
                    nc.vector.tensor_tensor(imp[:, :, :], iv, valid[:, i - 4], ALU.mult).then_inc(imp_step, 1)
                    dve.wait_ge(imp_step, n + 1)
                    nc.vector.tensor_tensor(impf[:, :, :], imp[:, :, :], force[:, i - 4], ALU.add).then_inc(imp_step, 1)
                    dve.wait_ge(imp_step, n + 2)
                    for g in range(2):
                        nc.vector.max(top[:, g, :], impf[:, g, :]).then_inc(imp_step, 1)
                    dve.wait_ge(imp_step, n + 4)
                    for g in range(2):
                        nc.vector.match_replace(rep[:, g, :], top[:, g, :], impf[:, g, :], -5.0).then_inc(rep_ready, 1)
                    dve.wait_ge(rep_ready, 2 * (i - 3))
                    nc.vector.tensor_tensor(same[:, :, :], rep[:, :, :], impf[:, :, :], ALU.is_equal).then_inc(same_ready, 1)
                    dve.wait_ge(same_ready, i - 3)
                    positive_wait(dve, selt_ready, i - 4)
                    nc.vector.tensor_scalar(uns[:, :, :], same[:, :, :], NEG, None, ALU.mult).then_inc(uns_ready, 1)

            def selection(i):
                dve.wait_ge(selt_ready, i - 3)
                nc.vector.tensor_copy(seln[0:NSEL, :, i * P:(i + 1) * P],
                                      p_x[3][0:NSEL, 0:2 * P].rearrange("p (a b) -> p a b", a=2)).then_inc(sel_ready, 1)

            soft(0)
            for i in range(TT):
                if i + 1 < TT:
                    soft(i + 1)
                normal(i)
                if i > 0:
                    result(i - 1)
                if i > 5:
                    selection(i - 2)
            result(TT - 1)
            selection(TT - 2)
            selection(TT - 1)

    sp.close()


class Steps:
    LAG = 2
    PV_LAG = 2

    def __init__(self, steps, proj=0):
        self.steps, self.proj = steps, proj
        self.n = len(steps)
        self.chunks = []
        self.first = []
        for s, st in enumerate(steps):
            self.first.append(len(self.chunks))
            nb = st["hi"] - st["lo"]
            for b in range(0, nb, 4):
                self.chunks.append((s, b, min(4, nb - b)))
        self.first.append(len(self.chunks))
        self.m = len(self.chunks)

    def order(self, proj=True):
        pending = []
        users = [("scores", s) for s in range(self.n)] + [("proj", i) for i in range(self.proj if proj else 0)]
        tail = max(len(users), self.n + self.LAG)
        for u in range(tail):
            flush = self.proj and proj and u == len(users) - 1
            if flush:
                while pending:
                    yield ("values", pending.pop(0))
            if u < len(users):
                yield users[u]
            s = u - self.LAG
            if 0 <= s < self.n:
                for m in range(self.first[s], self.first[s + 1]):
                    yield ("turn", m)
                    pending.append(m)
                    if len(pending) > self.PV_LAG:
                        yield ("values", pending.pop(0))
        while pending:
            yield ("values", pending.pop(0))

    def last_chunk(self, m):
        s = self.chunks[m][0]
        return s if self.first[s + 1] == m + 1 else None


class Softmax:

    def __init__(self, core, sp, tag, sched):
        self.core, self.nc, self.sched = core, core.nc, sched
        self.p = sp.sb("probs", [P, 4, SEQ])
        self.pth = sp.sb("probs_t_hi", [P, 4, CW], F32R)
        self.ptl = sp.sb("probs_t_lo", [P, 4, CW], F32R)
        self.nmx = sp.sb("neg_max", [P, 8])
        self.rs = sp.sb("row_sum", [P, 8])
        self.ri = sp.sb("row_inv", [P, 8])
        self.os = sp.sb("o_sum", [P, 8, 64])
        self.p_s = [sp.ps(f"scores{b}", [P, 2 * CW]) for b in range(2)]
        self.p_t = [sp.ps(f"turned{b}", [P, CW]) for b in range(2)]
        self.p_o = [sp.ps(f"o{b}", [P, CW]) for b in range(2)]
        S = lambda n: core.sem(f"{tag}_{n}")
        self.scores_ready = S("scores_ready")
        self.max_ready = S("max_ready")
        self.exp_done = S("exp_done")
        self.turned = S("turned")
        self.hi_done = S("probs_hi_done")
        self.lo_done = S("probs_lo_done")
        self.values_done = S("values_done")
        self.inv_ready = S("inv_ready")
        self.sum_done = S("sum_done")
        self.out_done = S("out_done")

    def turn(self, pe, ident, it, m):
        sc, (s, b0, nb) = self.sched, self.sched.chunks[m]
        pe.wait_ge(self.exp_done, sc.n * it + s + 1)
        positive_wait(pe, self.lo_done, sc.m * it + m + 1 - 2)
        for b in range(nb):
            last = pe.transpose(self.p_t[m % 2][:, b * P:(b + 1) * P],
                                self.p[:, s % 4, (b0 + b) * P:(b0 + b + 1) * P], ident[:, :])
        last.then_inc(self.turned, 1)

    def values(self, pe, it, m):
        sc, (s, b0, nb) = self.sched, self.sched.chunks[m]
        st = sc.steps[s]
        pe.wait_ge(self.lo_done, sc.m * it + m + 1)
        if b0 == 0:
            positive_wait(pe, self.sum_done, sc.n * it + s + 1 - 2)
        nblk = st["hi"] - st["lo"]
        for b in range(nb):
            c = slice(b * P, (b + 1) * P)
            v, ends = st["v"](st["lo"] + b0 + b), b0 + b == nblk - 1
            pe.matmul(self.p_o[s % 2][:, 0:P], self.pth[:, m % 4, c], v, start=b0 + b == 0, stop=ends,
                      skip_group_check=True)
            last = pe.matmul(self.p_o[s % 2][:, 0:64], self.ptl[:, m % 4, c], v[:, 0:64], start=False, stop=ends,
                             skip_group_check=True)
        last.then_inc(self.values_done, 1)

    def exp(self, act, it, s):
        sc = self.sched
        w = (sc.steps[s]["hi"] - sc.steps[s]["lo"]) * P
        act.wait_ge(self.max_ready, sc.n * it + s + 1)
        t = sc.m * it + (sc.first[s - 3] if s >= 4 else sc.first[s - 3 + sc.n] - sc.m)
        positive_wait(act, self.turned, t)
        positive_wait(act, self.out_done, sc.n * it + s + 1 - 8)
        self.nc.scalar.activation(self.p[:, s % 4, 0:w], self.p_s[s % 2][:, 0:w], ACT.Exp,
                                  bias=self.nmx[:, s % 8:s % 8 + 1],
                                  accum_out=self.rs[:, s % 8:s % 8 + 1]).then_inc(self.exp_done, 1)

    def hi(self, act, it, m):
        sc, (s, b0, nb) = self.sched, self.sched.chunks[m]
        act.wait_ge(self.turned, sc.m * it + m + 1)
        positive_wait(act, self.values_done, sc.m * it + m + 1 - 4)
        self.nc.scalar.activation(self.pth[:, m % 4, 0:nb * P], self.p_t[m % 2][:, 0:nb * P],
                                  ACT.Copy).then_inc(self.hi_done, 1)

    def maximum(self, dve, it, s):
        sc = self.sched
        w = (sc.steps[s]["hi"] - sc.steps[s]["lo"]) * P
        dve.wait_ge(self.scores_ready, sc.n * it + s + 1)
        self.nc.vector.tensor_reduce(self.nmx[:, s % 8:s % 8 + 1], self.p_s[s % 2][:, 0:w], AX.X, ALU.max,
                                     negate=True).then_inc(self.max_ready, 1)

    def lo(self, dve, it, m):
        sc, (s, b0, nb) = self.sched, self.sched.chunks[m]
        dve.wait_ge(self.hi_done, sc.m * it + m + 1)
        self.nc.vector.tensor_tensor(self.ptl[:, m % 4, 0:nb * P], self.p_t[m % 2][:, 0:nb * P],
                                     self.pth[:, m % 4, 0:nb * P].bitcast(F32), ALU.subtract).then_inc(self.lo_done, 1)

    def totals(self, dve, it, m, s):
        sc = self.sched
        dve.wait_ge(self.values_done, sc.m * it + m + 1)
        dve.wait_ge(self.exp_done, sc.n * it + s + 1)
        self.nc.vector.reciprocal(self.ri[:, s % 8:s % 8 + 1], self.rs[:, s % 8:s % 8 + 1]).then_inc(self.inv_ready, 1)
        self.nc.vector.tensor_reduce(self.os[:, s % 8, :], self.p_o[s % 2][:, 0:P].rearrange("p (c d) -> p d c", c=2),
                                     AX.X, ALU.add).then_inc(self.sum_done, 1)
        dve.wait_ge(self.inv_ready, sc.n * it + s + 1)
        dve.wait_ge(self.sum_done, sc.n * it + s + 1)


def nsa_attention(core, ch, mix, gates, onsa, seln):
    nc, d = core.nc, core.d
    sp = Space(nc, "nsa2")
    ident = sp.sb("ident", [P, P])
    identb = sp.sb("ident_bf", [P, P], BF16)
    masks = sp.sb("masks", [P, 2, P], BF16)
    erow = sp.sb("block_rows", [17, SEQ], BF16)
    alib = sp.sb("alibi", [17, 2, SEQ], BF16)
    selb = sp.sb("alibi_selected", [17, 2, SEQ], BF16)
    q = [[sp.sb(f"q{g}_{p}", [P, SEQ], F32R) for p in ("hi", "lo")] for g in range(2)]
    k = [[sp.sb(f"k{b}_{p}", [P, SEQ], F32R) for p in ("hi", "lo")] for b in range(2)]
    kf = sp.sb("k_scaled", [P, 2, SEQ])
    v = sp.sb("v_hi_lo", [P, TT, 4 * P], F32R)
    v_parts = v[:, :, :].rearrange("p t (b c d) -> p t b c d", b=4, c=2)
    v_mix = mix[:, :, C_VS:C_VS + 2 * P].rearrange("p t (b d) -> p t b d", b=4)
    rg = sp.sb("row_scale", [P, 8])

    def bias_of(g, br):
        return lambda tok: (selb if br == 0 else alib)[:, g, tok]

    steps = []
    for br in range(2):
        for n in range(TT):
            for g, i in ((0, TT - 1 - n), (1, n)):
                lo = 0 if br == 0 else max(0, i - WIN_TILES)
                steps.append(dict(i=i, g=g, br=br, lo=lo, hi=i + 1, q=q[g], k=k[br], bias=bias_of(g, br),
                                  v=lambda kb, g=g, br=br: v[:, kb, (2 * br + g) * P:(2 * br + g + 1) * P]))
    sched = Steps(steps)
    sm = Softmax(core, sp, "nsa2", sched)
    NJ = 4
    S = lambda n: core.sem(f"nsa2_{n}")
    consts_in, alib_in, zeroed = S("consts_in"), S("alibi_in"), S("zeroed")
    kf_ready, kv_hi, kv_lo = S("kf_ready"), S("kv_hi"), S("kv_lo")
    q_hi, q_lo, sel_ready, rg_ready = S("q_hi"), S("q_lo"), S("sel_bias_ready"), S("row_scale_ready")

    def loop(eng, body):
        body(0)
        with eng.Fori(1, NJ) as j:
            body(j)

    with nc.Block("nsa2_blk") as block:

        @block.sync
        def _(sync):
            for dst, name in ((ident, "ident"), (identb, "ident_bf"), (masks, "masks"), (erow, "block_rows")):
                sync.dma_start(dst[:], d[name]).then_inc(consts_in, 16)

            def load(j):
                positive_wait(sync, sm.scores_ready, sched.n * j)
                sync.dma_start(alib[:, :, :], d["alibi"][bass.ds(j, 1)].rearrange("a p g t -> (a p) g t")).then_inc(alib_in, 16)

            loop(sync, load)

        @block.gpsimd
        def _(pool):
            for g in range(2):
                for part in range(2):
                    r = slice(64 * (1 - g), 64 * (1 - g) + 64)
                    nc.gpsimd.memset(q[g][part][r, :].bitcast(F32), 0.0).then_inc(zeroed, 1)
            pool.wait_ge(zeroed, 4)
            for br in range(2):
                pool.wait_ge(kv_hi, br + 1)
                nc.gpsimd.tensor_tensor(k[br][1][:, :], kf[:, br, :], k[br][0][:, :].bitcast(F32),
                                        ALU.subtract).then_inc(kv_lo, 1)
            pool.wait_ge(kv_hi, 3)
            nc.gpsimd.tensor_tensor(v_parts[:, :, :, 1], v_mix, v_parts[:, :, :, 0].bitcast(F32),
                                    ALU.subtract).then_inc(kv_lo, 1)
            pool.wait_ge(kv_lo, 3)

            def heads(j):
                for g in range(2):
                    r = slice(64 * g, 64 * g + 64)
                    pool.wait_ge(q_hi, 2 * j + g + 1)
                    positive_wait(pool, q_lo, 2 * j + g)
                    nc.gpsimd.tensor_tensor(q[g][1][r, :].unsqueeze(1), ch[r, bass.ds(j, 1), :],
                                            q[g][0][r, :].bitcast(F32).unsqueeze(1), ALU.subtract).then_inc(q_lo, 1)
                pool.wait_ge(q_lo, 2 * j + 2)
                pool.wait_ge(alib_in, 16 * j + 16)
                nc.gpsimd.tensor_tensor(selb[:, :, :], alib[:, :, :], seln[:, :, :], ALU.add).then_inc(sel_ready, 1)
                pool.wait_ge(sel_ready, j + 1)

            loop(pool, heads)

        @block.tensor
        def _(pe):
            pe.wait_ge(consts_in, 64)
            pe.wait_ge(zeroed, 4)
            pe.wait_ge(kv_lo, 3)

            def scores(j, s):
                st = steps[s]
                if s == 0:
                    pe.wait_ge(sel_ready, j + 1)
                positive_wait(pe, sm.exp_done, sched.n * j + s + 1 - 2)
                tok = slice(st["i"] * P, st["i"] * P + P)
                w = (st["hi"] - st["lo"]) * P
                for c in range(0, w, CW):
                    e = min(w, c + CW)
                    keys = slice(st["lo"] * P + c, st["lo"] * P + e)
                    out = sm.p_s[s % 2][:, c:e]
                    pe.matmul(out, st["bias"](tok), erow[:, keys], start=True, stop=False)
                    if st["br"] == 1 and st["i"] >= WIN_TILES and c == 0:
                        pe.matmul(out[:, 0:P], identb[:, :], masks[:, 1, :], start=False, stop=False)
                    if e == w:
                        pe.matmul(out[:, e - c - P:e - c], identb[:, :], masks[:, 0, :], start=False, stop=False)
                    last = mm3(pe, out, tuple(x[:, tok] for x in st["q"]), tuple(x[:, keys] for x in st["k"]), False, True)
                last.then_inc(sm.scores_ready, 1)

            def heads(j):
                for what, n in sched.order():
                    if what == "scores":
                        scores(j, n)
                    elif what == "turn":
                        sm.turn(pe, ident, j, n)
                    else:
                        sm.values(pe, j, n)

            loop(pe, heads)

        @block.scalar
        def _(act):
            for br in range(2):
                act.wait_ge(kf_ready, br + 1)
                nc.scalar.activation(k[br][0][:, :], kf[:, br, :], ACT.Copy).then_inc(kv_hi, 1)
            nc.scalar.activation(v_parts[:, :, :, 0], v_mix, ACT.Copy).then_inc(kv_hi, 1)

            def heads(j):
                positive_wait(act, sm.scores_ready, sched.n * j)
                for g in range(2):
                    r = slice(64 * g, 64 * g + 64)
                    nc.scalar.activation(q[g][0][r, :].unsqueeze(1), ch[r, bass.ds(j, 1), :], ACT.Copy).then_inc(q_hi, 1)
                for what, n in sched.order():
                    if what == "scores":
                        for m in (range(sched.first[n - 2], sched.first[n - 1]) if n >= 2 else ()):
                            sm.hi(act, j, m)
                        sm.exp(act, j, n)
                for m in range(sched.first[sched.n - 2], sched.m):
                    sm.hi(act, j, m)

            loop(act, heads)

        @block.vector
        def _(dve):
            for br in range(2):
                nc.vector.tensor_scalar(kf[:, br, :], ch[:, T_KS + br, :], DH ** -0.5, None, ALU.mult).then_inc(kf_ready, 1)

            def out_step(j, m, s):
                st = steps[s]
                sm.totals(dve, j, m, s)
                i, g = st["i"], st["g"]
                col = 8 * (st["br"] + 1) + g
                dve_gate = gates[:, i, bass.ds(2 * j + col, 1)]
                nc.vector.tensor_tensor(rg[:, s % 8:s % 8 + 1], sm.ri[:, s % 8:s % 8 + 1], dve_gate,
                                        ALU.mult).then_inc(rg_ready, 1)
                dve.wait_ge(rg_ready, sched.n * j + s + 1)
                dst = onsa[:, i, bass.ds(2 * j * DH + g * DH, DH)]
                nc.vector.scalar_tensor_tensor(out=dst, in0=sm.os[:, s % 8, :], scalar=rg[:, s % 8:s % 8 + 1],
                                               in1=dst, op0=ALU.mult, op1=ALU.add).then_inc(sm.out_done, 1)

            def heads(j):
                for what, n in sched.order():
                    if what == "scores":
                        sm.maximum(dve, j, n)
                    elif what == "turn":
                        sm.lo(dve, j, n)
                    elif sched.last_chunk(n) is not None:
                        out_step(j, n, sched.last_chunk(n))

            loop(dve, heads)

    sp.close()


def close_layer(core, tag, o_of, gate_of, extra_of, w_dram, res_dram, gb_dram, xh=None, xl=None, out_of=None):
    nc, d = core.nc, core.d
    sp = Space(nc, tag)
    GW = o_of(0).shape[-1]
    ident = sp.sb("ident", [P, P])
    w_raw = sp.sb("w_raw", [P, 2, DM])
    wh = sp.sb("w_hi", [P, KT, DM], F32R)
    wl = sp.sb("w_lo", [P, KT, DM], F32R)
    gb = sp.sb("ln_gb", [P, 2, DM])
    gate = sp.sb("gate", [P, 2, GW])
    oc = sp.sb("o", [P, 2, DM])
    oth = sp.sb("o_t_hi", [P, 2, KT, P], F32R)
    otl = sp.sb("o_t_lo", [P, 2, KT, P], F32R)
    res = sp.sb("res", [P, 2, DM])
    z = res
    st = sp.sb("bn_stats", [P, 2, 6])
    mv = sp.sb("bn_mv", [P, 2])
    ve = sp.sb("var_eps", [P, 1])
    nh = sp.sb("neg_half", [P, 1])
    rstd = sp.sb("rstd", [P, 1])
    y = w_raw
    p_t = [sp.ps(f"turned{b}", [P, CW]) for b in range(2)]
    p_y = [sp.ps(f"y{b}", [P, DM]) for b in range(2)]
    p_x = [sp.ps(f"xt{b}", [P, CW]) for b in range(2)]
    S = lambda n: core.sem(f"{tag}_{n}")
    consts_in = S("consts_in")
    w_in, w_hi, w_lo = [S("w_in0"), S("w_in1")], S("w_hi"), S("w_lo")
    half_ready = S("half_ready")
    o_in, res_in = [S("o_in0"), S("o_in1")], [S("res_in0"), S("res_in1")]
    per_o = 16 if extra_of is None else 32
    oc_ready, t_ready, hi_done, lo_done = S("oc_ready"), S("t_ready"), S("hi_done"), S("lo_done")
    y_ready, z_ready, bn_ready, ve_ready, rstd_ready = S("y_ready"), S("z_ready"), S("bn_ready"), S("ve_ready"), S("rstd_ready")
    zn_ready, zg_ready, out_ready = S("zn_ready"), S("zg_ready"), S("out_ready")
    stored = [S("stored0"), S("stored1")]
    x_t, x_hi, x_lo = S("x_turned"), S("x_hi_done"), S("x_lo_done")
    nxt = xh is not None

    with nc.Block(f"{tag}_blk") as block:

        @block.sync
        def _(sync):
            sync.dma_start(ident[:, :], d["ident"]).then_inc(consts_in, 16)

            def o_tile(i):
                b = i % 2
                positive_wait(sync, t_ready, 2 * (i - 1))
                sync.dma_start(gate[:, b, :], gate_of(i)).then_inc(o_in[b], 16)
                if extra_of is not None:
                    sync.dma_start(oc[:, b, GW:DM], extra_of(i)).then_inc(o_in[b], 16)

            def res_tile(i):
                b = i % 2
                positive_wait(sync, out_ready, i - 1)
                sync.dma_start(res[:, b, :], res_dram[i]).then_inc(res_in[b], 16)

            o_tile(0)
            for k in range(KT):
                positive_wait(sync, w_lo, k - 1)
                sync.dma_start(w_raw[:, k % 2, :], w_dram[k * P:(k + 1) * P, :]).then_inc(w_in[k % 2], 16)
                if k == 1:
                    o_tile(1)
            sync.dma_start(gb[:, :, :], gb_dram).then_inc(consts_in, 16)
            res_tile(0)
            res_tile(1)
            o_tile(2)
            for i in range(TT):
                if i + 3 < TT:
                    o_tile(i + 3)
                if i >= 1 and i + 1 < TT:
                    res_tile(i + 1)
                sync.wait_ge(out_ready, i + 1)
                sync.dma_start(out_of(i), y[:, i % 2, :]).then_inc(stored[i % 2], 16)
            for b in range(2):
                sync.wait_ge(stored[b], 16 * (TT // 2))

        @block.gpsimd
        def _(pool):
            nc.gpsimd.memset(nh[:, :], -0.5).then_inc(half_ready, 1)
            for k in range(KT):
                pool.wait_ge(w_hi, k + 1)
                nc.gpsimd.tensor_tensor(wl[:, k, :], w_raw[:, k % 2, :], wh[:, k, :].bitcast(F32),
                                        ALU.subtract).then_inc(w_lo, 1)
            pool.wait_ge(half_ready, 1)
            pool.wait_ge(consts_in, 32)
            for i in range(TT):
                pool.wait_ge(ve_ready, i + 1)
                nc.gpsimd.tensor_tensor(rstd[:, :], ve[:, :], nh[:, :], ALU.pow).then_inc(rstd_ready, 1)
                pool.wait_ge(zn_ready, i + 1)
                nc.gpsimd.tensor_tensor(z[:, i % 2, :], z[:, i % 2, :], gb[:, 0, :], ALU.mult).then_inc(zg_ready, 1)
                pool.wait_ge(zg_ready, i + 1)
                positive_wait(pool, stored[i % 2], 16 * (i // 2))
                if nxt:
                    positive_wait(pool, x_t, 2 * (i - 1))
                nc.gpsimd.tensor_tensor(y[:, i % 2, :], z[:, i % 2, :], gb[:, 1, :], ALU.add).then_inc(out_ready, 1)

        @block.tensor
        def _(pe):
            pe.wait_ge(consts_in, 16)

            def turn_o(i):
                pe.wait_ge(oc_ready, i + 1)
                for hf in range(2):
                    positive_wait(pe, lo_done, 2 * i + hf - 1)
                    for k in range(4):
                        last = pe.transpose(p_t[hf][:, k * P:(k + 1) * P],
                                            oc[:, i % 2, (4 * hf + k) * P:(4 * hf + k + 1) * P], ident[:, :])
                    last.then_inc(t_ready, 1)

            def products(i):
                pe.wait_ge(lo_done, 2 * i + 2)
                positive_wait(pe, z_ready, i - 1)
                for k in range(KT):
                    if i == 0:
                        pe.wait_ge(w_lo, k + 1)
                    for c in range(2):
                        cs = slice(c * CW, (c + 1) * CW)
                        last = mm3(pe, p_y[i % 2][:, cs], (oth[:, i % 2, k, :], otl[:, i % 2, k, :]),
                                   (wh[:, k, cs], wl[:, k, cs]), k == 0, k == KT - 1)
                last.then_inc(y_ready, 1)

            def turn_x(i):
                pe.wait_ge(out_ready, i + 1)
                for hf in range(2):
                    positive_wait(pe, x_lo, 2 * i + hf - 1)
                    for k in range(4):
                        last = pe.transpose(p_x[hf][:, k * P:(k + 1) * P],
                                            y[:, i % 2, (4 * hf + k) * P:(4 * hf + k + 1) * P], ident[:, :])
                    last.then_inc(x_t, 1)

            turn_o(0)
            turn_o(1)
            for i in range(TT):
                products(i)
                if i + 2 < TT:
                    turn_o(i + 2)
                if nxt and i > 1:
                    turn_x(i - 2)
            if nxt:
                turn_x(TT - 2)
                turn_x(TT - 1)

        @block.scalar
        def _(act):
            for k in range(KT):
                act.wait_ge(w_in[k % 2], 16 * (k // 2 + 1))
                nc.scalar.activation(wh[:, k, :], w_raw[:, k % 2, :], ACT.Copy).then_inc(w_hi, 1)

            def hi_o(i):
                for hf in range(2):
                    act.wait_ge(t_ready, 2 * i + hf + 1)
                    positive_wait(act, y_ready, i - 1)
                    nc.scalar.activation(oth[:, i % 2, 4 * hf:4 * hf + 4, :],
                                         p_t[hf][:, :].rearrange("p (a b) -> p a b", a=4), ACT.Copy).then_inc(hi_done, 1)

            def hi_x(i):
                for hf in range(2):
                    act.wait_ge(x_t, 2 * i + hf + 1)
                    nc.scalar.activation(xh[:, 4 * hf:4 * hf + 4, i * P:(i + 1) * P],
                                         p_x[hf][:, :].rearrange("p (a b) -> p a b", a=4), ACT.Copy).then_inc(x_hi, 1)

            hi_o(0)
            hi_o(1)
            for i in range(TT):
                if i + 2 < TT:
                    hi_o(i + 2)
                if nxt and i > 1:
                    hi_x(i - 2)
            if nxt:
                hi_x(TT - 2)
                hi_x(TT - 1)

        @block.vector
        def _(dve):
            def gated(i):
                dve.wait_ge(o_in[i % 2], per_o * (i // 2 + 1))
                positive_wait(dve, t_ready, 2 * (i - 1))
                nc.vector.tensor_tensor(oc[:, i % 2, 0:GW], o_of(i), gate[:, i % 2, :], ALU.mult).then_inc(oc_ready, 1)

            def lo_o(i):
                positive_wait(dve, y_ready, i - 1)
                for hf in range(2):
                    dve.wait_ge(hi_done, 2 * i + hf + 1)
                    ks = slice(4 * hf, 4 * hf + 4)
                    nc.vector.tensor_tensor(otl[:, i % 2, ks, :], p_t[hf][:, :].rearrange("p (a b) -> p a b", a=4),
                                            oth[:, i % 2, ks, :].bitcast(F32), ALU.subtract).then_inc(lo_done, 1)

            def lo_x(i):
                for hf in range(2):
                    dve.wait_ge(x_hi, 2 * i + hf + 1)
                    ks, tok = slice(4 * hf, 4 * hf + 4), slice(i * P, (i + 1) * P)
                    nc.vector.tensor_tensor(xl[:, ks, tok], p_x[hf][:, :].rearrange("p (a b) -> p a b", a=4),
                                            xh[:, ks, tok].bitcast(F32), ALU.subtract).then_inc(x_lo, 1)

            def layer_norm(i):
                b = i % 2
                dve.wait_ge(y_ready, i + 1)
                dve.wait_ge(res_in[b], 16 * (i // 2 + 1))
                nc.vector.scalar_tensor_tensor(out=z[:, b, :], in0=res[:, b, :], scalar=ALPHA, in1=p_y[b][:, :],
                                               op0=ALU.mult, op1=ALU.add).then_inc(z_ready, 1)
                dve.wait_ge(z_ready, i + 1)
                for c in range(2):
                    nc.vector.bn_stats(st[:, c, :], z[:, b, c * CW:(c + 1) * CW]).then_inc(bn_ready, 1)
                dve.wait_ge(bn_ready, 3 * i + 2)
                nc.vector.bn_aggr(mv[:, :], st[:, :, :]).then_inc(bn_ready, 1)
                dve.wait_ge(bn_ready, 3 * i + 3)
                nc.vector.tensor_scalar(ve[:, :], mv[:, 1:2], EPS, None, ALU.add).then_inc(ve_ready, 1)
                dve.wait_ge(rstd_ready, i + 1)
                nc.vector.tensor_scalar(z[:, b, :], z[:, b, :], mv[:, 0:1], rstd[:, 0:1], ALU.subtract,
                                        ALU.mult).then_inc(zn_ready, 1)

            gated(0)
            lo_o(0)
            gated(1)
            lo_o(1)
            gated(2)
            for i in range(TT):
                if i + 2 < TT:
                    lo_o(i + 2)
                if i + 3 < TT:
                    gated(i + 3)
                layer_norm(i)
                if nxt and i > 1:
                    lo_x(i - 2)
            if nxt:
                lo_x(TT - 2)
                lo_x(TT - 1)

    sp.close()


def latents(core, lat, cqh, cql, ckh, ckl, k_bufs):
    nc, d = core.nc, core.d
    sp = Space(nc, "lat")
    CWL = QL + KVL
    ident = sp.sb("ident", [P, P])
    g = sp.sb("norm_g", [P, CWL])
    trig = sp.sb("cos_sin", [P, 2, TT, ROPE // 2])
    sq = sp.sb("square", [P, QL])
    ss = sp.sb("sum_sq", [P, TT, 2])
    ms = sp.sb("mean_sq", [P, TT, 2])
    nh = sp.sb("neg_half", [P, TT, 2])
    rstd = sp.sb("rstd", [P, TT, 2])
    cn = sp.sb("c_norm", [P, 2, CWL])
    t1 = sp.sb("rope_tmp", [P, 4, TT, ROPE // 2])
    kr = sp.sb("k_rope", [P, TT, 4, 2, ROPE // 2])
    p_q = [sp.ps(f"q{b}", [P, CW]) for b in range(2)]
    p_k = [sp.ps(f"k{b}", [P, CW]) for b in range(2)]
    p_r = sp.ps("rope", [P, 2 * CW])
    S = lambda n: core.sem(f"lat_{n}")
    consts_in, half_ready, sq_done, ms_ready, rstd_ready = S("consts_in"), S("half_ready"), S("sq_done"), S("ms_ready"), S("rstd_ready")
    cn_ready, c_turned, c_hi, c_lo = S("cn_ready"), S("c_turned"), S("c_hi"), S("c_lo")
    rope_step, rope_ready, r_turned, r_hi, r_lo = S("rope_step"), S("rope_ready"), S("r_turned"), S("r_hi"), S("r_lo")

    with nc.Block("lat_blk") as block:

        @block.sync
        def _(sync):
            for dst, name in ((ident, "ident"), (g, "latent_norms"), (trig, "cos_sin_tok")):
                sync.dma_start(dst[:], d[name]).then_inc(consts_in, 16)

        @block.gpsimd
        def _(pool):
            nc.gpsimd.memset(nh[:, :, :], -0.5).then_inc(half_ready, 1)
            pool.wait_ge(half_ready, 1)
            pool.wait_ge(ms_ready, 2)
            nc.gpsimd.tensor_tensor(rstd[:, :, :], ms[:, :, :], nh[:, :, :], ALU.pow).then_inc(rstd_ready, 1)

        @block.tensor
        def _(pe):
            pe.wait_ge(consts_in, 48)
            pe.wait_ge(rope_step, 6)
            pe.wait_ge(rope_ready, 3)
            for i in range(TT):
                last = pe.transpose(p_r[:, i * P:(i + 1) * P], kr[:, i], ident[:, :])
            last.then_inc(r_turned, 1)
            for i in range(TT):
                pe.wait_ge(cn_ready, 2 * i + 2)
                positive_wait(pe, c_lo, 2 * (i - 1))
                for k in range(QT):
                    pe.transpose(p_q[i % 2][:, k * P:(k + 1) * P], cn[:, i % 2, k * P:(k + 1) * P], ident[:, :])
                for k in range(KVT):
                    last = pe.transpose(p_k[i % 2][:, k * P:(k + 1) * P],
                                        cn[:, i % 2, QL + k * P:QL + (k + 1) * P], ident[:, :])
                last.then_inc(c_turned, 1)

        @block.scalar
        def _(act):
            n = 0
            for i in range(TT):
                for c, (a, b) in enumerate(((0, QL), (QL, QL + KVL))):
                    positive_wait(act, sq_done, n)
                    nc.scalar.activation(sq[:, 0:b - a], lat[:, i, a:b], ACT.Square,
                                         accum_out=ss[:, i, c:c + 1]).then_inc(sq_done, 1)
                    n += 1
            act.wait_ge(r_turned, 1)
            for half, kb in ((1, k_bufs[0]), (0, k_bufs[1])):
                r = slice(64 * half, 64 * half + 64)
                nc.scalar.activation(kb[0][r, :], p_r[r, :], ACT.Copy).then_inc(r_hi, 1)
            for i in range(TT):
                tok = slice(i * P, (i + 1) * P)
                act.wait_ge(c_turned, i + 1)
                nc.scalar.activation(cqh[:, :, tok], p_q[i % 2][:, 0:QL].rearrange("p (a b) -> p a b", a=QT),
                                     ACT.Copy).then_inc(c_hi, 1)
                nc.scalar.activation(ckh[:, :, tok], p_k[i % 2][:, 0:KVL].rearrange("p (a b) -> p a b", a=KVT),
                                     ACT.Copy).then_inc(c_hi, 1)

        @block.vector
        def _(dve):
            dve.wait_ge(consts_in, 48)
            x1, x2 = lat[:, :, CWL:CWL + 16], lat[:, :, CWL + 16:CWL + 32]
            cos, sin = trig[:, 0], trig[:, 1]
            for n, (x, t) in enumerate(((x1, cos), (x2, sin), (x2, cos), (x1, sin))):
                nc.vector.tensor_tensor(t1[:, n], x, t, ALU.mult).then_inc(rope_step, 1)
            dve.wait_ge(rope_step, 4)
            for c in range(2):
                nc.vector.tensor_tensor(kr[:, :, 0, c, :], t1[:, 2 * c], t1[:, 2 * c + 1],
                                        ALU.subtract if c == 0 else ALU.add).then_inc(rope_step, 1)
            dve.wait_ge(rope_step, 6)
            nc.vector.tensor_copy(kr[:, :, 1], kr[:, :, 0]).then_inc(rope_ready, 1)
            nc.vector.tensor_copy(kr[:, :, 2], kr[:, :, 0]).then_inc(rope_ready, 1)
            nc.vector.tensor_copy(kr[:, :, 3], kr[:, :, 0]).then_inc(rope_ready, 1)
            dve.wait_ge(sq_done, 2 * TT)
            for c, w in enumerate((QL, KVL)):
                nc.vector.tensor_scalar(ms[:, :, c], ss[:, :, c], 1.0 / w, EPS, ALU.mult, ALU.add).then_inc(ms_ready, 1)
            dve.wait_ge(rstd_ready, 1)

            def norm(i):
                positive_wait(dve, c_turned, i - 1)
                for c, (a, b) in enumerate(((0, QL), (QL, QL + KVL))):
                    nc.vector.scalar_tensor_tensor(out=cn[:, i % 2, a:b], in0=lat[:, i, a:b], scalar=rstd[:, i, c:c + 1],
                                                   in1=g[:, a:b], op0=ALU.mult, op1=ALU.mult).then_inc(cn_ready, 1)

            norm(0)
            for n, (half, kb) in enumerate(((1, k_bufs[0]), (0, k_bufs[1]))):
                r = slice(64 * half, 64 * half + 64)
                dve.wait_ge(r_hi, n + 1)
                nc.vector.tensor_tensor(kb[1][r, :], p_r[r, :], kb[0][r, :].bitcast(F32), ALU.subtract).then_inc(r_lo, 1)
            for i in range(TT):
                if i + 1 < TT:
                    norm(i + 1)
                tok = slice(i * P, (i + 1) * P)
                for c, (hi, lo, ps, w, nt) in enumerate(((cqh, cql, p_q, QL, QT), (ckh, ckl, p_k, KVL, KVT))):
                    dve.wait_ge(c_hi, 2 * i + c + 1)
                    nc.vector.tensor_tensor(lo[:, :, tok], ps[i % 2][:, 0:w].rearrange("p (a b) -> p a b", a=nt),
                                            hi[:, :, tok].bitcast(F32), ALU.subtract).then_inc(c_lo, 1)

    sp.close()


def mla_attention(core, cq, ck, kb, o_all):
    nc, d = core.nc, core.d
    sp = Space(nc, "mla")
    NP = MLA_H // 2
    WUQ, WUK, WV = QT * 2 * P, KVT * P, KVT * P
    WW = WUQ + WUK + WV
    ident = sp.sb("ident", [P, P])
    identb = sp.sb("ident_bf", [P, P], BF16)
    masks = sp.sb("masks", [P, 2, P], BF16)
    cs = sp.sb("rotation", [P, 2, SEQ])
    w_raw = sp.sb("w_raw", [P, WW])
    wh = sp.sb("w_hi", [P, WW], F32R)
    wl = sp.sb("w_lo", [P, WW], F32R)
    qf = sp.sb("q_rotated", [P, 2, SEQ])
    q = [[sp.sb(f"q{h}_{p}", [P, SEQ], F32R) for p in ("hi", "lo")] for h in range(2)]
    v = sp.sb("v_hi_lo", [P, TT, 2 * P], F32R)
    v_parts = v[:, :, :].rearrange("p t (h c d) -> p t h c d", h=2, c=2)

    steps = []
    for n in range(TT):
        for h, i in ((0, TT - 1 - n), (1, n)):
            steps.append(dict(i=i, h=h, lo=0, hi=i + 1,
                              v=lambda t, h=h: v[:, t, h * P:(h + 1) * P]))
    sched = Steps(steps, proj=4)
    sm = Softmax(core, sp, "mla", sched)
    S = lambda n: core.sem(f"mla_{n}")
    consts_in, w_in, w_hi, w_lo = S("consts_in"), S("w_in"), S("w_hi"), S("w_lo")
    proj_ready, proj_free = S("proj_ready"), S("proj_free")
    qf_ready, q_hi, q_lo, kv_hi = S("qf_ready"), S("q_hi"), S("q_lo"), S("kv_hi")

    def loop(eng, body):
        body(0, False)
        with eng.Fori(1, NP - 1) as it:
            body(it, False)
        body(NP - 1, True)

    with nc.Block("mla_blk") as block:

        @block.sync
        def _(sync):
            for dst, name in ((ident, "ident"), (identb, "ident_bf"), (masks, "masks"), (cs, "rotation")):
                sync.dma_start(dst[:], d[name]).then_inc(consts_in, 16)
            sync.dma_start(w_raw[:, :], d["w_heads"][0]).then_inc(w_in, 16)

            def load(it, last):
                if last:
                    return
                sync.wait_ge(w_lo, it + 1)
                src = d["w_heads"][bass.ds(it + 1, 1)].rearrange("a p c -> (a p) c")
                sync.dma_start(w_raw[:, :], src).then_inc(w_in, 16)

            loop(sync, load)

        @block.gpsimd
        def _(pool):
            def w_split(n):
                pool.wait_ge(w_hi, n + 1)
                nc.gpsimd.tensor_tensor(wl[:, :], w_raw[:, :], wh[:, :].bitcast(F32), ALU.subtract).then_inc(w_lo, 1)

            def q_split(n):
                for h in range(2):
                    pool.wait_ge(q_hi, 2 * n + h + 1)
                    nc.gpsimd.tensor_tensor(q[h][1][:, :], qf[:, h, :], q[h][0][:, :].bitcast(F32),
                                            ALU.subtract).then_inc(q_lo, 1)

            w_split(0)
            q_split(0)

            def pair(it, last):
                if not last:
                    w_split(it + 1)
                    q_split(it + 1)

            loop(pool, pair)

        @block.tensor
        def _(pe):
            pe.wait_ge(consts_in, 64)

            def project(n, i):
                ps = sm.p_s[i % 2]
                if i == 0:
                    pe.wait_ge(w_lo, n + 1)
                if i < 2:
                    positive_wait(pe, sm.exp_done, sched.n * n - 1 + i)
                else:
                    pe.wait_ge(qf_ready, 2 * n + i - 1)
                if i < 3:
                    kt, src = (QT, cq) if i < 2 else (KVT, ck)
                    for c in range(2):
                        tok = slice(c * CW, (c + 1) * CW)
                        for k in range(kt):
                            col = (k * 2 * P + i * P) if i < 2 else WUQ + k * P
                            last = mm3(pe, ps[:, tok], (wh[:, col:col + P], wl[:, col:col + P]),
                                       (src[0][:, k, tok], src[1][:, k, tok]), k == 0, k == kt - 1)
                else:
                    for t in range(TT):
                        tok = slice(t * P, (t + 1) * P)
                        for k in range(KVT):
                            col = WUQ + WUK + k * P
                            last = mm3(pe, ps[:, tok], (ck[0][:, k, tok], ck[1][:, k, tok]),
                                       (wh[:, col:col + P], wl[:, col:col + P]), k == 0, k == KVT - 1)
                last.then_inc(proj_ready, 1)

            def scores(it, s):
                st = steps[s]
                if s == 0:
                    pe.wait_ge(q_lo, 2 * it + 2)
                    pe.wait_ge(proj_free, 2 * it + 1)
                if s == 1:
                    pe.wait_ge(proj_free, 2 * it + 2)
                if s >= 2:
                    pe.wait_ge(sm.exp_done, sched.n * it + s - 1)
                tok = slice(st["i"] * P, st["i"] * P + P)
                w = st["hi"] * P
                for c in range(0, w, CW):
                    e = min(w, c + CW)
                    out = sm.p_s[s % 2][:, c:e]
                    last = mm3(pe, out, tuple(x[:, tok] for x in q[st["h"]]), tuple(x[:, c:e] for x in kb[st["h"]]),
                               True, e != w)
                    if e == w:
                        last = pe.matmul(out[:, e - c - P:e - c], identb[:, :], masks[:, 0, :], start=False, stop=True)
                last.then_inc(sm.scores_ready, 1)

            def pair(it, last):
                for what, n in sched.order(proj=not last):
                    if what == "scores":
                        scores(it, n)
                    elif what == "proj":
                        project(it + 1, n)
                    elif what == "turn":
                        sm.turn(pe, ident, it, n)
                    else:
                        sm.values(pe, it, n)

            for i in range(4):
                project(0, i)
            loop(pe, pair)

        @block.scalar
        def _(act):
            def w_split(n):
                act.wait_ge(w_in, 16 * n + 16)
                positive_wait(act, proj_ready, 4 * n)
                nc.scalar.activation(wh[:, :], w_raw[:, :], ACT.Copy).then_inc(w_hi, 1)

            def projected(n, i):
                if i < 2:
                    act.wait_ge(qf_ready, 2 * n + i + 1)
                    nc.scalar.activation(q[i][0][:, :], qf[:, i, :], ACT.Copy).then_inc(q_hi, 1)
                    return
                act.wait_ge(proj_ready, 4 * n + i + 1)
                ps = sm.p_s[i % 2]
                if i == 2:
                    nc.scalar.activation(kb[0][0][0:64, :], ps[0:64, :], ACT.Copy).then_inc(kv_hi, 1)
                    nc.scalar.activation(kb[1][0][64:P, :], ps[64:P, :], ACT.Copy).then_inc(kv_hi, 1)
                else:
                    positive_wait(act, sm.values_done, sched.m * n)
                    nc.scalar.activation(v_parts[:, :, :, 0], ps[:, :].rearrange("p (t h d) -> p t h d", t=TT, h=2),
                                         ACT.Copy).then_inc(kv_hi, 1)

            def pair(it, last):
                for what, n in sched.order(proj=not last):
                    if what == "scores":
                        for m in (range(sched.first[n - 2], sched.first[n - 1]) if n >= 2 else ()):
                            sm.hi(act, it, m)
                        sm.exp(act, it, n)
                        if n == sched.n // 2 and not last:
                            w_split(it + 1)
                    elif what == "turn" and sched.chunks[n][0] >= sched.n - 2:
                        sm.hi(act, it, n)
                    elif what == "proj":
                        projected(it + 1, n)

            w_split(0)
            for i in range(4):
                projected(0, i)
            loop(act, pair)

        @block.vector
        def _(dve):
            dve.wait_ge(consts_in, 64)

            def projected(n, i):
                ps = sm.p_s[i % 2]
                if i < 2:
                    dve.wait_ge(proj_ready, 4 * n + i + 1)
                    positive_wait(dve, q_lo, 2 * n + i - 1)
                    nc.vector.tensor_tensor(qf[:, i, :], ps[:, :], cs[:, i, :], ALU.mult).then_inc(qf_ready, 1)
                    return
                if i == 2:
                    for h in range(2):
                        r = slice(64 * h, 64 * h + 64)
                        dve.wait_ge(kv_hi, 3 * n + h + 1)
                        ins = nc.vector.tensor_tensor(kb[h][1][r, :], ps[r, :], kb[h][0][r, :].bitcast(F32), ALU.subtract)
                else:
                    dve.wait_ge(kv_hi, 3 * n + 3)
                    ins = nc.vector.tensor_tensor(v_parts[:, :, :, 1], ps[:, :].rearrange("p (t h d) -> p t h d", t=TT, h=2),
                                                  v_parts[:, :, :, 0].bitcast(F32), ALU.subtract)
                ins.then_inc(proj_free, 1)

            def out_step(it, m, s):
                st = steps[s]
                sm.totals(dve, it, m, s)
                nc.vector.tensor_scalar(o_all[:, st["i"], bass.ds(it * 2 * VD + st["h"] * VD, VD)],
                                        sm.os[:, s % 8, :], sm.ri[:, s % 8:s % 8 + 1], None,
                                        ALU.mult).then_inc(sm.out_done, 1)

            def pair(it, last):
                for what, n in sched.order(proj=not last):
                    if what == "scores":
                        sm.maximum(dve, it, n)
                    elif what == "turn":
                        sm.lo(dve, it, n)
                    elif what == "proj":
                        projected(it + 1, n)
                    elif sched.last_chunk(n) is not None:
                        out_step(it, n, sched.last_chunk(n))

            for i in range(4):
                projected(0, i)
            loop(dve, pair)

    sp.close()


def build(nc, dram, out, stop_after=None):
    core = Core(nc, dram)
    gate_dram = nc.dram_tensor("silu_gates_scratch", (TT, P, 2 * CW), F32).ap()
    og_dram = nc.dram_tensor("gla_out_scratch", (TT, P, CW), F32).ap()
    x1_dram = nc.dram_tensor("x1_scratch", (TT, P, DM), F32).ap()
    z_dram = nc.dram_tensor("silu_z_scratch", (TT, P, DM), F32).ap()
    x_dram = dram["x"].rearrange("(t p) c -> t p c", p=P)
    out_tiles = out[0].rearrange("(t p) c -> t p c", p=P)

    base = Space(nc, "base")
    region = base.sb("region", [P, TT * W_LAT])
    onsa = region[:, 0:TT * CW].rearrange("p (t c) -> p t c", t=TT)
    gates = region[:, TT * CW:TT * (CW + 24)].rearrange("p (t c) -> p t c", t=TT)
    seln = region[0:17, TT * (CW + 24):TT * (CW + 24) + SEQ].bitcast(BF16).rearrange("p (g t) -> p g t", g=2)
    lat = region[:, :].rearrange("p (t c) -> p t c", t=TT)

    l0 = Space(nc, "l0")
    ch = l0.sb("ch", [P, N_CH, SEQ])
    mix = l0.sb("mix", [P, TT, W_MIX])
    gv_sp = Space(nc, "gv")
    gv = gv_sp.sb("gv", [P, TT, CW])
    xs = Space(nc, "x0t")
    xh = xs.sb("hi", [P, KT, SEQ], F32R)
    xl = xs.sb("lo", [P, KT, SEQ], F32R)
    runs = [
        dict(kind="ch", first=0, count=3, col=0, width=CW,
             move=lambda ps, i, t: (ch[:, bass.ds(4 * i + t // 2, 1), (t % 2) * CW:(t % 2 + 1) * CW],
                                    ps[:, t:t + 1, :])),
        dict(kind="tm", first=3, count=1, col=3 * CW, width=CW,
             silu=lambda t: gate_dram[t, :, 0:CW]),
        dict(kind="tm", first=4, count=1, col=4 * CW, width=CW,
             silu=lambda t: gate_dram[t, :, CW:2 * CW]),
        dict(kind="tm", first=5, count=1, col=5 * CW, width=CW,
             move=lambda ps, i, t: (gv[:, t, :], ps[:, t, :])),
        dict(kind="tm", first=6, count=1, col=6 * CW, width=W_MIX,
             move=lambda ps, i, t: (mix[:, t, :], ps[:, t, 0:W_MIX])),
    ]
    project(core, "l0p", dram["w0"], runs, xh, xl, dram["x_t"])
    xs.close()

    gla(core, ch, mix, gv, og_dram, gate_dram)
    gv_sp.close()
    compressed(core, ch, mix, gates, onsa, seln)
    nsa_attention(core, ch, mix, gates, onsa, seln)
    l0.close()

    l1 = Space(nc, "l1")
    xh = l1.sb("x_hi", [P, KT, SEQ], F32R)
    xl = l1.sb("x_lo", [P, KT, SEQ], F32R)
    close_layer(core, "out0", lambda i: onsa[:, i, :], lambda i: gate_dram[i, :, 0:CW], lambda i: og_dram[i],
                dram["w_out0"], x_dram, dram["ln0"], xh, xl, lambda i: x1_dram[i])
    if stop_after == "x1":
        dump(core, out, [(xh[:, 3, :].bitcast(F32), 1), (xl[:, 3, :].bitcast(F32), 2)], [(x1_dram[5], 0), (x1_dram[0], 3)])
        return

    core.retire_semaphores()

    runs = [
        dict(kind="tm", first=0, count=1, col=W_LAT, width=CW, silu=lambda t: z_dram[t, :, 0:CW]),
        dict(kind="tm", first=1, count=1, col=W_LAT + CW, width=CW, silu=lambda t: z_dram[t, :, CW:2 * CW]),
        dict(kind="tm", first=2, count=1, col=0, width=CW,
             move=lambda ps, i, t: (lat[:, t, 0:CW], ps[:, t, :])),
        dict(kind="tm", first=3, count=1, col=CW, width=W_LAT - CW,
             move=lambda ps, i, t: (lat[:, t, CW:W_LAT], ps[:, t, 0:W_LAT - CW])),
    ]
    project(core, "l1p", dram["w1"], runs, xh, xl)
    l1.close()

    ospace = Space(nc, "oall")
    o_all = ospace.sb("o", [P, TT, DM])
    lspace = Space(nc, "l1b")
    cq = [lspace.sb(f"cq_{p}", [P, QT, SEQ], F32R) for p in ("hi", "lo")]
    ck = [lspace.sb(f"ckv_{p}", [P, KVT, SEQ], F32R) for p in ("hi", "lo")]
    kb = [[lspace.sb(f"k{h}_{p}", [P, SEQ], F32R) for p in ("hi", "lo")] for h in range(2)]
    latents(core, lat, cq[0], cq[1], ck[0], ck[1], kb)
    mla_attention(core, cq, ck, kb, o_all)
    lspace.close()

    close_layer(core, "out1", lambda i: o_all[:, i, :], lambda i: z_dram[i], None,
                dram["w_out1"], x1_dram, dram["ln1"], out_of=lambda i: out_tiles[i])
    ospace.close()
    base.close()


def dump(core, out, tiles, drams=(), tag=""):
    nc = core.nc
    done = core.sem("dump_done" + tag)
    with nc.Block("dump" + tag) as block:
        @block.sync
        def _(sync):
            for ap, row in tiles:
                r = int(row)
                col = int((row - r) * 1024)
                w = ap.shape[-1]
                sync.dma_start(out[0, r * P:r * P + ap.shape[0], col:col + w], ap).then_inc(done, 16)
            for ap, row in drams:
                sync.dma_start(out[0, row * P:(row + 1) * P, 0:ap.shape[-1]], ap).then_inc(done, 16)
            sync.wait_ge(done, 16 * (len(tiles) + len(drams)))


SLOT_HEAD = [g * 4 + j for j in range(4) for g in range(2)]


SLOPES = np.array([2.0 ** -(h + 1) for h in SLOT_HEAD])


def w0_columns():
    nq, nkv, ng, nz = 0, 512, 1280, 1304
    gq, gk, gv, ga, gz = 1816, 2072, 2328, 2840, 2856
    cols = []
    for h in SLOT_HEAD:
        cols += range(nq + h * 64, nq + h * 64 + 64)
    kv = lambda br, j: list(range(nkv + (br * 2 + j) * 128, nkv + (br * 2 + j) * 128 + 128))
    cols += kv(0, 0) + kv(0, 1) + kv(1, 0) + kv(2, 0)
    cols += range(gq, gq + 512)
    for h in SLOT_HEAD:
        cols += range(nz + h * 64, nz + h * 64 + 64)
    cols += range(gz, gz + 512)
    cols += range(gv, gv + 512)
    cols += kv(1, 1) + kv(2, 1)
    cols += [ng + br * 8 + h for br in range(3) for h in SLOT_HEAD]
    cols += range(ga, ga + 16)
    return np.array(cols)


def layout(inp):
    a = {}
    x = np.asarray(inp["x"])[0]
    a["x"] = x
    a["x_t"] = x.T
    a["w0"] = np.asarray(inp["e_w_in"])[0][:, w0_columns()]
    a["gla_wg"] = np.concatenate([np.asarray(inp["e_gla_w_gate"])[0], np.asarray(inp["e_gla_b_gate"])], 0)
    a["gla_norm"] = np.broadcast_to(np.asarray(inp["e_gla_norm"]), (P, P))
    a["ident"] = np.eye(P, dtype=np.float32)
    s_, t_ = np.arange(P)[:, None], np.arange(P)[None, :]
    same = s_ // GC == t_ // GC
    a["tri_suffix"] = np.concatenate([same & (s_ <= t_), same & (s_ > t_)], 1).astype(np.float32) / 16.0
    causal = (np.arange(GC)[None, :] >= (np.arange(P) % GC)[:, None]).astype(np.int32)
    a["gla_causal"] = np.broadcast_to(causal[:, None, :], (P, GLA_H, GC))
    w1 = np.asarray(inp["e_cmp_w1"])[0].reshape(2, CMP_BLOCK // 2, 2, DH, P)
    a["cmp_w1"] = w1.transpose(2, 3, 0, 1, 4).reshape(P, 2, CMP_BLOCK // 2, P)
    a["cmp_w2"] = np.asarray(inp["e_cmp_w2"])[0].transpose(1, 0, 2)
    pe = np.asarray(inp["e_cmp_pe"])[0].transpose(2, 0, 1)
    a["cmp_pe_t"] = np.concatenate([pe, np.roll(pe, -1, 2)], 0)
    q, m = np.arange(P)[:, None, None], np.arange(-56, 64)[None, None, :]
    slope = SLOPES[None, :, None]
    a["cmp_bias"] = np.where(q >= CMP_STRIDE * m + CMP_BLOCK - 1, slope * (CMP_STRIDE * m), NEG).astype(np.float32)
    start, sel = CMP_STRIDE * np.arange(NCMP)[:, None], 64 * np.arange(NSEL)[None, :]
    ov = np.clip(np.minimum(start + CMP_BLOCK, sel + 64) - np.maximum(start, sel), 0, None) / CMP_BLOCK
    ov[N_CMP:] = 0
    z = np.zeros_like(ov)
    a["overlap"] = np.block([[ov, z], [z, ov]]).astype(np.float32)
    pos = np.arange(4 * P, SEQ).reshape(4, P).T[:, :, None, None]
    cur, jj = pos // 64, np.arange(NSEL)[None, None, None, :]
    shape = (P, 4, 2, NSEL)
    a["valid"] = np.broadcast_to((jj <= cur).astype(np.float32), shape)
    forced = (jj == 0) | (jj == cur) | (jj == cur - 1)
    a["force"] = np.broadcast_to(np.where(jj > cur, -1.0, np.where(forced, 1000.0, 0.0)).astype(np.float32), shape)
    wo = np.asarray(inp["e_w_out"])[0]
    rows = [h * 64 + c for h in SLOT_HEAD for c in range(64)] + list(range(512, 1024))
    a["w_out0"] = wo[rows]
    a["w_out1"] = np.asarray(inp["o_w_out"])[0]
    a["ln0"] = np.broadcast_to(np.stack([np.asarray(inp["e_ln_g"])[0], np.asarray(inp["e_ln_b"])[0]]), (P, 2, DM))
    a["ln1"] = np.broadcast_to(np.stack([np.asarray(inp["o_ln_g"])[0], np.asarray(inp["o_ln_b"])[0]]), (P, 2, DM))
    a["w1"] = np.asarray(inp["o_w_in"])[0]
    norms = np.concatenate([np.asarray(inp["o_q_norm"])[0], np.asarray(inp["o_kv_norm"])[0]])
    a["latent_norms"] = np.broadcast_to(norms, (P, QL + KVL))
    half = ROPE // 2
    freqs = np.exp(np.float32(-np.log(10000.0)) * np.arange(half, dtype=np.float32) * np.float32(2.0) / np.float32(ROPE))
    ang = np.arange(SEQ, dtype=np.float32)[:, None] * freqs[None, :].astype(np.float32)
    cos, sin = np.cos(ang).astype(np.float32), np.sin(ang).astype(np.float32)
    a["cos_sin_tok"] = np.stack([cos, sin]).reshape(2, TT, P, half).transpose(2, 0, 1, 3)
    sc = np.float32(MLA_SCALE)
    nope = np.full((NOPE, SEQ), sc, np.float32)
    cc, sg = np.concatenate([cos.T, cos.T]) * sc, np.concatenate([-sin.T, sin.T]) * sc
    a["rotation"] = np.stack([np.concatenate([nope, cc, sg]), np.concatenate([cc, sg, nope])], 1)
    uq = np.asarray(inp["o_w_uq"])[0].reshape(QT, P, MLA_H, NOPE + ROPE)
    ukv = np.asarray(inp["o_w_ukv"])[0].reshape(KVT, P, MLA_H, NOPE + VD)
    qn, r1, r2 = uq[..., :NOPE], uq[..., NOPE:NOPE + half], uq[..., NOPE + half:]
    qa = np.concatenate([qn, r1, r2, r2, r1], -1)[:, :, 0::2]
    qb = np.concatenate([r1, r2, r2, r1, qn], -1)[:, :, 1::2]
    wq = np.concatenate([qa, qb], -1).transpose(2, 1, 0, 3).reshape(MLA_H // 2, P, QT * 2 * P)
    wk = ukv[..., :NOPE].reshape(KVT, P, MLA_H // 2, 2 * NOPE).transpose(2, 1, 0, 3).reshape(MLA_H // 2, P, KVT * P)
    wv = ukv[..., NOPE:].reshape(KVT, P, MLA_H // 2, 2 * VD).transpose(2, 1, 0, 3).reshape(MLA_H // 2, P, KVT * P)
    a["w_heads"] = np.concatenate([wq, wk, wv], -1)
    bf = np.dtype("bfloat16")
    a["ident_bf"] = np.eye(P).astype(bf)
    qq, kk = np.arange(P)[:, None], np.arange(P)[None, :]
    a["masks"] = np.stack([np.where(kk > qq, NEG, 0.0), np.where(kk <= qq, NEG, 0.0)], 1).astype(bf)
    keys = np.arange(SEQ)
    a["block_rows"] = np.concatenate([(keys[None, :] // 64 == np.arange(NSEL)[:, None]), (keys % 64)[None, :]], 0).astype(bf)
    rel = 64.0 * (np.arange(NSEL)[:, None] - 2 * (keys // P)[None, :])
    rel = np.concatenate([rel, np.ones((1, SEQ))], 0)
    a["alibi"] = (SLOPES.reshape(4, 1, 2, 1) * rel[None, :, None, :]).astype(bf)
    return {k: np.ascontiguousarray(v) for k, v in a.items()}


STOP = None


def kernel(**inputs):
    import concourse.bacc as _bacc
    from concourse.bass_utils import run_bass_kernel_spmd as _run

    nc = _bacc.Bacc("TRN2", target_bir_lowering=False, num_devices=1)
    arrays, dram = {}, {}
    for name, a in layout(inputs).items():
        arrays[f"in_{name}_dram"] = a
        dram[name] = nc.dram_tensor(f"in_{name}_dram", a.shape, mybir.dt.from_np(a.dtype), kind="ExternalInput").ap()
    out = nc.dram_tensor("out_0_dram", (1, SEQ, DM), F32, kind="ExternalOutput").ap()
    build(nc, dram, out, STOP)
    r = _run(nc, [arrays], core_ids=[0])
    return r.results[0]["out_0_dram"]
```
